# Optimizing a Trainium2 kernel written in Bass

```python
import math
import jax, jax.numpy as jnp
from jax import lax
import numpy as np

D_MODEL = 1024
BATCH = 1
SEQ = 512
DEPTH = 1

SSD_EXPAND = 2
D_INNER = SSD_EXPAND * D_MODEL
SSD_HEAD_DIM = 64
SSD_HEADS = D_INNER // SSD_HEAD_DIM
SSD_GROUPS = 8
D_STATE = 128
SSD_CONV = 4
SSD_CHUNK = 128
SSD_CONV_DIM = D_INNER + 2 * SSD_GROUPS * D_STATE
SSD_NORM_GROUP = D_INNER // SSD_GROUPS
ATTN_WINDOWS = (128, 512, 2048)
ATTN_DILATIONS = (1, 4, 16)
ATTN_N_GROUPS = 3
ATTN_HEADS_PER_GROUP = 8
ATTN_HEAD_DIM = 64
ATTN_BLOCK = 128
ATTN_WIDTH = ATTN_N_GROUPS * ATTN_HEADS_PER_GROUP * ATTN_HEAD_DIM
ATTN_OUT = ATTN_HEADS_PER_GROUP * ATTN_HEAD_DIM
D_FF = 2816
FFN_CONV = 3
EPS = 1e-6
IN_WIDTHS = (D_INNER, SSD_CONV_DIM, SSD_HEADS, ATTN_WIDTH, ATTN_WIDTH, ATTN_WIDTH, D_MODEL, D_MODEL)
IN_SPLITS = tuple(sum(IN_WIDTHS[:i + 1]) for i in range(len(IN_WIDTHS) - 1))
D_IN_PROJ = sum(IN_WIDTHS)


def rms_norm(x, g):
    xf = x.astype(jnp.float32)
    y = xf * lax.rsqrt(jnp.mean(xf * xf, axis=-1, keepdims=True) + EPS)
    return (y * g.astype(jnp.float32)).astype(x.dtype)

def causal_dwconv(x, w, bias):
    K = w.shape[0]
    s = x.shape[1]
    xp = jnp.pad(x, ((0, 0), (K - 1, 0), (0, 0)))
    out = bias
    for i in range(K):
        out = out + xp[:, i:i + s] * w[i]
    return out

def ssd_chunked(xs, dt, A, Bm, Cm):
    b, s, H, P = xs.shape
    G, N = Bm.shape[2], Bm.shape[3]
    K = H // G
    Q = SSD_CHUNK
    c = s // Q
    X = (xs * dt[..., None]).reshape(b, c, Q, G, K, P)
    a = (dt * A).reshape(b, c, Q, G, K).transpose(0, 1, 3, 4, 2)
    a_cs = jnp.cumsum(a, axis=-1)
    Bc = Bm.reshape(b, c, Q, G, N)
    Cc = Cm.reshape(b, c, Q, G, N)
    causal = jnp.tril(jnp.ones((Q, Q), dtype=bool))
    seg = a_cs[..., :, None] - a_cs[..., None, :]
    Ldec = jnp.exp(jnp.where(causal, seg, -jnp.inf))
    CB = jnp.einsum('bclgn,bcsgn->bcgls', Cc, Bc)
    y_diag = jnp.einsum('bcgkls,bcsgkp->bclgkp', CB[:, :, :, None] * Ldec, X)
    decay_states = jnp.exp(a_cs[..., -1:] - a_cs)
    states = jnp.einsum('bclgn,bcgkl,bclgkp->bcgkpn', Bc, decay_states, X)
    chunk_decay = jnp.exp(a_cs[..., -1])

    def step(carry, inp):
        st, dec = inp
        return carry * dec[..., None, None] + st, carry

    init = jnp.zeros((b, G, K, P, N), jnp.float32)
    _, prev = lax.scan(step, init, (jnp.moveaxis(states, 1, 0), jnp.moveaxis(chunk_decay, 1, 0)))
    prev = jnp.moveaxis(prev, 0, 1)
    y_off = jnp.einsum('bclgn,bcgkpn,bcgkl->bclgkp', Cc, prev, jnp.exp(a_cs))
    return (y_diag + y_off).reshape(b, s, H, P)

def ssd_branch(z, xbc, dt_raw, conv_w, conv_b, dt_bias, a_log, d_skip, norm_g):
    b, s, _ = z.shape
    f32 = jnp.float32
    xbc = jax.nn.silu(causal_dwconv(xbc, conv_w, conv_b))
    xs, Bm, Cm = jnp.split(xbc, (D_INNER, D_INNER + SSD_GROUPS * D_STATE), axis=-1)
    xs = xs.reshape(b, s, SSD_HEADS, SSD_HEAD_DIM).astype(f32)
    Bm = Bm.reshape(b, s, SSD_GROUPS, D_STATE).astype(f32)
    Cm = Cm.reshape(b, s, SSD_GROUPS, D_STATE).astype(f32)
    dt = jax.nn.softplus(dt_raw.astype(f32) + dt_bias.astype(f32))
    A = -jnp.exp(a_log.astype(f32))
    y = ssd_chunked(xs, dt, A, Bm, Cm) + d_skip.astype(f32)[:, None] * xs
    y = y.reshape(b, s, D_INNER) * jax.nn.silu(z.astype(f32))
    y = rms_norm(y.reshape(b, s, SSD_GROUPS, SSD_NORM_GROUP), norm_g.reshape(SSD_GROUPS, SSD_NORM_GROUP))
    return y.reshape(b, s, D_INNER).astype(z.dtype)

def dilated_window_attention(q, k, v, dil, n_back):
    b, s, h, hd = q.shape
    L = s // dil
    nb = -(-L // ATTN_BLOCK)
    Lp = nb * ATTN_BLOCK

    def to_sub(t):
        t = t.reshape(b, L, dil, h, hd).transpose(0, 2, 1, 3, 4).reshape(b * dil, L, h, hd)
        t = jnp.pad(t, ((0, 0), (0, Lp - L), (0, 0), (0, 0)))
        return t.reshape(b * dil, nb, ATTN_BLOCK, h, hd)

    def with_prev(t):
        prev = jnp.pad(t, ((0, 0), (1, 0), (0, 0), (0, 0), (0, 0)))[:, :-1]
        return jnp.concatenate([prev, t], axis=2)

    qb = to_sub(q)
    kc = with_prev(to_sub(k))
    vc = with_prev(to_sub(v))
    scores = jnp.einsum('znqhd,znkhd->znhqk', qb, kc) * (hd ** -0.5)
    qi = jnp.arange(ATTN_BLOCK)[:, None]
    ki = jnp.arange(2 * ATTN_BLOCK)[None, :]
    dist = ATTN_BLOCK + qi - ki
    band = (dist >= 0) & (dist <= n_back)
    key_pos = (jnp.arange(nb)[:, None, None] - 1) * ATTN_BLOCK + ki[None]
    mask = band[None] & (key_pos >= 0)
    scores = jnp.where(mask[None, :, None], scores, -jnp.inf)
    m = jnp.max(scores, axis=-1, keepdims=True)
    p = jnp.exp(scores - m)
    den = jnp.sum(p, axis=-1, keepdims=True)
    o = jnp.einsum('znhqk,znkhd->znqhd', p / den, vc)
    lse = (m + jnp.log(den))[..., 0]
    o = o.reshape(b, dil, Lp, h, hd)[:, :, :L].transpose(0, 2, 1, 3, 4).reshape(b, s, h, hd)
    lse = lse.transpose(0, 1, 3, 2).reshape(b, dil, Lp, h)[:, :, :L].transpose(0, 2, 1, 3).reshape(b, s, h)
    return o, lse

def attn_branch(q, k, v, q_norm_g, k_norm_g):
    b, s, _ = q.shape
    f32 = jnp.float32
    shp = (b, s, ATTN_N_GROUPS, ATTN_HEADS_PER_GROUP, ATTN_HEAD_DIM)
    qn = rms_norm(q.reshape(shp), q_norm_g).astype(f32)
    kn = rms_norm(k.reshape(shp), k_norm_g).astype(f32)
    vv = v.reshape(shp).astype(f32)
    outs, lses = [], []
    for gi in range(ATTN_N_GROUPS):
        o, lse = dilated_window_attention(qn[:, :, gi], kn[:, :, gi], vv[:, :, gi],
                                          ATTN_DILATIONS[gi], ATTN_WINDOWS[gi] // ATTN_DILATIONS[gi])
        outs.append(o)
        lses.append(lse)
    wts = jax.nn.softmax(jnp.stack(lses, axis=0), axis=0)
    o = jnp.einsum('gbsh,gbshd->bshd', wts, jnp.stack(outs, axis=0))
    return o.reshape(b, s, ATTN_OUT).astype(q.dtype)

def first_inputs(seed: int = 0) -> dict:
    key = jax.random.key(seed)
    ks = jax.random.split(key, 20)
    f32 = jnp.float32

    def dense(k, shape, fan_in):
        return jax.random.normal(k, shape, f32) * fan_in ** -0.5

    def gain(k, shape):
        return 1.0 + 0.05 * jax.random.normal(k, shape, f32)

    x = jax.random.normal(ks[0], (BATCH, SEQ, D_MODEL), f32)
    norm1_g = gain(ks[1], (DEPTH, D_MODEL))
    w_in = dense(ks[2], (DEPTH, D_MODEL, D_IN_PROJ), D_MODEL)
    ssd_conv_w = dense(ks[3], (DEPTH, SSD_CONV, SSD_CONV_DIM), SSD_CONV)
    ssd_conv_b = 0.02 * jax.random.normal(ks[4], (DEPTH, SSD_CONV_DIM), f32)
    dt0 = jnp.exp(jax.random.uniform(ks[5], (DEPTH, SSD_HEADS), f32, math.log(1e-3), math.log(1e-1)))
    dt_bias = dt0 + jnp.log(-jnp.expm1(-dt0))
    a_log = jnp.log(jax.random.uniform(ks[6], (DEPTH, SSD_HEADS), f32, 1.0, 16.0))
    d_skip = 1.0 + 0.1 * jax.random.normal(ks[7], (DEPTH, SSD_HEADS), f32)
    ssd_norm_g = gain(ks[8], (DEPTH, D_INNER))
    w_ssd_proj = dense(ks[9], (DEPTH, D_INNER, D_MODEL), D_INNER)
    q_norm_g = gain(ks[10], (DEPTH, ATTN_HEAD_DIM))
    k_norm_g = gain(ks[11], (DEPTH, ATTN_HEAD_DIM))
    w_attn_proj = dense(ks[12], (DEPTH, ATTN_OUT, D_MODEL), ATTN_OUT)
    w_out = dense(ks[13], (DEPTH, D_MODEL, D_MODEL), D_MODEL)
    norm2_g = gain(ks[14], (DEPTH, D_MODEL))
    w_up = dense(ks[15], (DEPTH, D_MODEL, 2 * D_FF), D_MODEL)
    ffn_conv_w = dense(ks[16], (DEPTH, FFN_CONV, 2 * D_FF), FFN_CONV)
    ffn_conv_b = 0.02 * jax.random.normal(ks[17], (DEPTH, 2 * D_FF), f32)
    w_down = dense(ks[18], (DEPTH, D_FF, D_MODEL), D_FF)
    return {'x': x, 'norm1_g': norm1_g, 'w_in': w_in, 'ssd_conv_w': ssd_conv_w, 'ssd_conv_b': ssd_conv_b,
            'dt_bias': dt_bias, 'a_log': a_log, 'd_skip': d_skip, 'ssd_norm_g': ssd_norm_g,
            'w_ssd_proj': w_ssd_proj, 'q_norm_g': q_norm_g, 'k_norm_g': k_norm_g,
            'w_attn_proj': w_attn_proj, 'w_out': w_out, 'norm2_g': norm2_g, 'w_up': w_up,
            'ffn_conv_w': ffn_conv_w, 'ffn_conv_b': ffn_conv_b, 'w_down': w_down}

def first_block(x, norm1_g, w_in, ssd_conv_w, ssd_conv_b, dt_bias, a_log, d_skip, ssd_norm_g,
              w_ssd_proj, q_norm_g, k_norm_g, w_attn_proj, w_out, norm2_g, w_up,
              ffn_conv_w, ffn_conv_b, w_down):
    for l in range(DEPTH):
        h = rms_norm(x, norm1_g[l])
        proj = h @ w_in[l]
        z, xbc, dt_raw, q, k, v, g_ssd, g_attn = jnp.split(proj, IN_SPLITS, axis=-1)
        y_ssd = ssd_branch(z, xbc, dt_raw, ssd_conv_w[l], ssd_conv_b[l], dt_bias[l], a_log[l],
                           d_skip[l], ssd_norm_g[l])
        y_attn = attn_branch(q, k, v, q_norm_g[l], k_norm_g[l])
        merged = (jax.nn.sigmoid(g_ssd) * (y_ssd @ w_ssd_proj[l])
                  + jax.nn.sigmoid(g_attn) * (y_attn @ w_attn_proj[l]))
        x = x + merged @ w_out[l]
        h2 = rms_norm(x, norm2_g[l])
        u = causal_dwconv(h2 @ w_up[l], ffn_conv_w[l], ffn_conv_b[l])
        u_gate, u_val = jnp.split(u, 2, axis=-1)
        x = x + (jax.nn.silu(u_gate) * u_val) @ w_down[l]
    return x


DEPTH_2 = 2

MIX_WIDTH = D_MODEL
GDN_HEADS = 4
GDN_HEAD_DIM = 128
GDN_WIDTH = GDN_HEADS * GDN_HEAD_DIM
GDN_CONV = 4
GDN_CHUNK = 64
NSA_HEADS = 8
NSA_KV_HEADS = 2
NSA_HEAD_DIM = 64
NSA_WIDTH = NSA_HEADS * NSA_HEAD_DIM
NSA_KV_WIDTH = NSA_KV_HEADS * NSA_HEAD_DIM
CMP_LEN = 32
CMP_STRIDE = 16
CMP_HIDDEN = 2 * NSA_HEAD_DIM
SEL_BLOCK = 64
N_SELECT = 16
WINDOW = 512
Q_BLOCK = 128
ROPE_THETA = 500000.0
ROT_DIM = NSA_HEAD_DIM // 4
N_ADA = 9
NORM_EPS = 1e-6
IN_SIZES = (3 * GDN_WIDTH, GDN_WIDTH, GDN_HEADS, GDN_HEADS,
            NSA_WIDTH, NSA_KV_WIDTH, NSA_KV_WIDTH, NSA_KV_WIDTH,
            NSA_KV_WIDTH, NSA_KV_WIDTH, NSA_KV_WIDTH, 3 * NSA_HEADS)
IN_WIDTH = sum(IN_SIZES)


def rms_norm_2(x, g):
    xf = x.astype(jnp.float32)
    y = xf * lax.rsqrt(jnp.mean(xf * xf, axis=-1, keepdims=True) + NORM_EPS)
    return (y * g.astype(jnp.float32)).astype(x.dtype)

def l2_norm(x):
    xf = x.astype(jnp.float32)
    return xf * lax.rsqrt(jnp.sum(xf * xf, axis=-1, keepdims=True) + NORM_EPS)

def modulate(h, shift, scale):
    return h * (1.0 + scale[:, None, :]) + shift[:, None, :]

def swiglu(h, w_in, w_out):
    gate, up = jnp.split(h @ w_in, 2, axis=-1)
    return (jax.nn.silu(gate) * up) @ w_out

def split_cols(x, sizes):
    offs = [int(o) for o in np.cumsum(sizes)[:-1]]
    return jnp.split(x, offs, axis=-1)

def masked_softmax(s, mask):
    s = jnp.where(mask, s.astype(jnp.float32), -jnp.inf)
    m = jnp.max(s, axis=-1, keepdims=True)
    m = jnp.where(jnp.isfinite(m), m, 0.0)
    p = jnp.exp(s - m)
    return p / jnp.maximum(jnp.sum(p, axis=-1, keepdims=True), 1e-30)

def partial_rope(x, cos, sin):
    half = ROT_DIM // 2
    xf = x[..., :ROT_DIM].astype(jnp.float32)
    x1, x2 = xf[..., :half], xf[..., half:]
    rot = jnp.concatenate([x1 * cos - x2 * sin, x2 * cos + x1 * sin], axis=-1).astype(x.dtype)
    return jnp.concatenate([rot, x[..., ROT_DIM:]], axis=-1)

def causal_dwconv_2(x, w):
    k = w.shape[0]
    return lax.conv_general_dilated(
        x, w[:, None, :].astype(x.dtype), window_strides=(1,), padding=[(k - 1, 0)],
        dimension_numbers=("NWC", "WIO", "NWC"), feature_group_count=x.shape[-1])

def chunk_gated_delta_rule(q, k, v, g, beta):
    B, T, H, Dk = q.shape
    Dv = v.shape[-1]
    C = GDN_CHUNK
    N = T // C

    def chunks(t):
        t = t.astype(jnp.float32).reshape((B, N, C, H) + t.shape[3:])
        return jnp.moveaxis(t, (1, 3), (0, 2))

    qc, kc, vc, bc = chunks(q), chunks(k), chunks(v), chunks(beta)
    gc = jnp.cumsum(chunks(g), axis=-1)
    causal = jnp.tril(jnp.ones((C, C), dtype=bool))
    strict = jnp.tril(jnp.ones((C, C), dtype=bool), -1)
    decay = jnp.exp(jnp.where(causal, gc[..., :, None] - gc[..., None, :], -jnp.inf))
    kb = kc * bc[..., None]
    lower = jnp.where(strict, jnp.einsum("nbhcd,nbhsd->nbhcs", kb, kc) * decay, 0.0)
    rhs = jnp.concatenate([vc * bc[..., None], kb * jnp.exp(gc)[..., None]], axis=-1)
    sol = lax.linalg.triangular_solve(lower, rhs, left_side=True, lower=True, unit_diagonal=True)
    u, w = sol[..., :Dv], sol[..., Dv:]

    def step(S, xs):
        q_i, k_i, u_i, w_i, g_i, d_i = xs
        v_new = u_i - jnp.einsum("bhcd,bhdv->bhcv", w_i, S)
        attn = jnp.einsum("bhcd,bhsd->bhcs", q_i, k_i) * d_i
        o = (jnp.einsum("bhcd,bhdv->bhcv", q_i * jnp.exp(g_i)[..., None], S)
             + jnp.einsum("bhcs,bhsv->bhcv", attn, v_new))
        g_last = g_i[..., -1:]
        S = (S * jnp.exp(g_last)[..., None]
             + jnp.einsum("bhcd,bhcv->bhdv", k_i * jnp.exp(g_last - g_i)[..., None], v_new))
        return S, o

    S0 = jnp.zeros((B, H, Dk, Dv), jnp.float32)
    _, o = lax.scan(step, S0, (qc, kc, u, w, gc, decay))
    return jnp.moveaxis(o, (0, 2), (1, 3)).reshape(B, T, H, Dv)

def gated_deltanet(qkv, z, b_raw, a_raw, conv_w, a_log, dt_bias, norm_g):
    B, T, _ = qkv.shape
    qkv = jax.nn.silu(causal_dwconv_2(qkv, conv_w))
    q, k, v = jnp.split(qkv, 3, axis=-1)
    hd = (B, T, GDN_HEADS, GDN_HEAD_DIM)
    q = l2_norm(q.reshape(hd)) * (GDN_HEAD_DIM ** -0.5)
    k = l2_norm(k.reshape(hd))
    v = v.reshape(hd)
    beta = jax.nn.sigmoid(b_raw.astype(jnp.float32))
    g = -jnp.exp(a_log.astype(jnp.float32)) * jax.nn.softplus(a_raw.astype(jnp.float32) + dt_bias.astype(jnp.float32))
    o = chunk_gated_delta_rule(q, k, v, g, beta)
    o = rms_norm_2(o, norm_g) * jax.nn.silu(z.reshape(hd).astype(jnp.float32))
    return o.reshape(B, T, GDN_WIDTH).astype(qkv.dtype)

def native_sparse_attention(q, kc, vc, ks, vs, kw, vw, gate_raw, cos, sin,
                            pe_k, w1_k, w2_k, pe_v, w1_v, w2_v, out_norm_g):
    B, T, _ = q.shape
    Hq, G, dh = NSA_HEADS, NSA_KV_HEADS, NSA_HEAD_DIM
    R = Hq // G
    scale = dh ** -0.5
    q = partial_rope(q.reshape(B, T, Hq, dh), cos, sin).reshape(B, T, G, R, dh)
    heads = lambda t: t.reshape(B, T, G, dh)
    kc = partial_rope(heads(kc), cos, sin)
    ks = partial_rope(heads(ks), cos, sin)
    kw = partial_rope(heads(kw), cos, sin)
    vc, vs, vw = heads(vc), heads(vs), heads(vw)

    n_cmp = (T - CMP_LEN) // CMP_STRIDE + 1
    cmp_idx = np.arange(n_cmp)[:, None] * CMP_STRIDE + np.arange(CMP_LEN)[None, :]

    def compress(t, pe, w1, w2):
        blk = t[:, cmp_idx] + pe[:, None, :]
        blk = jnp.moveaxis(blk, 3, 2).reshape(B, n_cmp, G, CMP_LEN * dh)
        return jax.nn.silu(blk @ w1) @ w2

    k_cmp = compress(kc, pe_k, w1_k, w2_k)
    v_cmp = compress(vc, pe_v, w1_v, w2_v)
    cmp_end = jnp.asarray(cmp_idx[:, -1])

    n_blk = T // SEL_BLOCK
    n_sel = min(N_SELECT, n_blk)
    sel_start = np.arange(n_blk) * SEL_BLOCK
    overlap = jnp.asarray(((cmp_idx[:, :1] < sel_start[None, :] + SEL_BLOCK)
                           & (cmp_idx[:, -1:] >= sel_start[None, :])).astype(np.float32))
    blk_ids = jnp.arange(n_blk)
    ks_t = jnp.moveaxis(ks, 2, 1)
    vs_t = jnp.moveaxis(vs, 2, 1)
    b_ix = jnp.arange(B)[:, None, None, None]
    g_ix = jnp.arange(G)[None, :, None, None]
    kw_pad = jnp.pad(kw, ((0, 0), (WINDOW, 0), (0, 0), (0, 0)))
    vw_pad = jnp.pad(vw, ((0, 0), (WINDOW, 0), (0, 0), (0, 0)))
    gates = jax.nn.sigmoid(gate_raw.astype(jnp.float32)).reshape(B, T, G, R, 3)

    def one_block(i):
        s = i * Q_BLOCK
        t = s + jnp.arange(Q_BLOCK)
        qb = lax.dynamic_slice_in_dim(q, s, Q_BLOCK, axis=1)
        gb = lax.dynamic_slice_in_dim(gates, s, Q_BLOCK, axis=1)
        sc = jnp.einsum("bqgrd,bngd->bgrqn", qb, k_cmp) * scale
        p_cmp = masked_softmax(sc, cmp_end[None, :] <= t[:, None])
        o_cmp = jnp.einsum("bgrqn,bngd->bqgrd", p_cmp.astype(v_cmp.dtype), v_cmp)
        imp = jnp.einsum("bgrqn,nj->bgqj", p_cmp, overlap)
        cur = t[:, None] // SEL_BLOCK
        forced = (blk_ids == 0) | (blk_ids == cur) | (blk_ids == cur - 1)
        valid = blk_ids * SEL_BLOCK <= t[:, None]
        imp = jnp.where(forced, jnp.inf, jnp.where(valid, imp, -jnp.inf))
        _, top = lax.top_k(imp, n_sel)
        tok = (top[..., None] * SEL_BLOCK + jnp.arange(SEL_BLOCK)).reshape(B, G, Q_BLOCK, n_sel * SEL_BLOCK)
        k_sel = ks_t[b_ix, g_ix, tok]
        v_sel = vs_t[b_ix, g_ix, tok]
        ss = jnp.einsum("bqgrd,bgqld->bgrql", qb, k_sel) * scale
        p_sel = masked_softmax(ss, (tok <= t[:, None])[:, :, None])
        o_sel = jnp.einsum("bgrql,bgqld->bqgrd", p_sel.astype(v_sel.dtype), v_sel)
        k_win = lax.dynamic_slice_in_dim(kw_pad, s, WINDOW + Q_BLOCK, axis=1)
        v_win = lax.dynamic_slice_in_dim(vw_pad, s, WINDOW + Q_BLOCK, axis=1)
        kp = s - WINDOW + jnp.arange(WINDOW + Q_BLOCK)
        win_mask = (kp[None, :] <= t[:, None]) & (kp[None, :] > t[:, None] - WINDOW) & (kp[None, :] >= 0)
        sw = jnp.einsum("bqgrd,bkgd->bgrqk", qb, k_win) * scale
        p_win = masked_softmax(sw, win_mask)
        o_win = jnp.einsum("bgrqk,bkgd->bqgrd", p_win.astype(v_win.dtype), v_win)
        o = gb[..., 0:1] * o_cmp + gb[..., 1:2] * o_sel + gb[..., 2:3] * o_win
        o = rms_norm_2(o, out_norm_g)
        return o.reshape(B, Q_BLOCK, NSA_WIDTH)

    out = lax.map(one_block, jnp.arange(T // Q_BLOCK))
    return jnp.moveaxis(out, 0, 1).reshape(B, T, NSA_WIDTH).astype(q.dtype)

def token_mix(h, w_in, conv_w, a_log, dt_bias, gdn_norm_g, pe_k, w1_k, w2_k,
              pe_v, w1_v, w2_v, nsa_norm_g, w_out, cos, sin):
    (qkv, z, b_raw, a_raw, q_n, kc, vc, ks, vs, kw, vw, g_raw) = split_cols(h @ w_in, IN_SIZES)
    y_gdn = gated_deltanet(qkv, z, b_raw, a_raw, conv_w, a_log, dt_bias, gdn_norm_g)
    y_nsa = native_sparse_attention(q_n, kc, vc, ks, vs, kw, vw, g_raw, cos, sin,
                                    pe_k, w1_k, w2_k, pe_v, w1_v, w2_v, nsa_norm_g)
    return jnp.concatenate([y_gdn, y_nsa.astype(y_gdn.dtype)], axis=-1) @ w_out

def second_inputs(seed: int = 0) -> dict:
    key = jax.random.key(seed)
    ks = jax.random.split(key, 24)
    nrm = lambda k, shape, s: jax.random.normal(k, shape, jnp.float32) * s
    x = nrm(ks[0], (BATCH, SEQ, D_MODEL), 1.0)
    c = nrm(ks[1], (BATCH, D_MODEL), 1.0)
    positions = (jax.random.randint(ks[2], (BATCH, 1), 0, SEQ, dtype=jnp.int32)
                 + jnp.arange(SEQ, dtype=jnp.int32)[None, :])
    ada_w = nrm(ks[3], (DEPTH_2, D_MODEL, N_ADA * D_MODEL), 0.5 * D_MODEL ** -0.5)
    ada_b = nrm(ks[4], (DEPTH_2, N_ADA * D_MODEL), 0.02)
    norm_g = 1.0 + nrm(ks[5], (DEPTH_2, 3, D_MODEL), 0.02)
    ffn_w_in = nrm(ks[6], (DEPTH_2, 2, D_MODEL, 2 * D_FF), D_MODEL ** -0.5)
    ffn_w_out = nrm(ks[7], (DEPTH_2, 2, D_FF, D_MODEL), D_FF ** -0.5)
    mix_w_in = nrm(ks[8], (DEPTH_2, D_MODEL, IN_WIDTH), D_MODEL ** -0.5)
    gdn_conv_w = nrm(ks[9], (DEPTH_2, GDN_CONV, 3 * GDN_WIDTH), GDN_CONV ** -0.5)
    gdn_a_log = jnp.log(jax.random.uniform(ks[10], (DEPTH_2, GDN_HEADS), jnp.float32, 1.0, 16.0))
    dt = jnp.exp(jax.random.uniform(ks[11], (DEPTH_2, GDN_HEADS), jnp.float32, math.log(1e-3), math.log(1e-1)))
    gdn_dt_bias = dt + jnp.log(-jnp.expm1(-dt))
    gdn_norm_g = 1.0 + nrm(ks[12], (DEPTH_2, GDN_HEAD_DIM), 0.02)
    cmp_pe_k = nrm(ks[13], (DEPTH_2, CMP_LEN, NSA_HEAD_DIM), 0.1)
    cmp_w1_k = nrm(ks[14], (DEPTH_2, CMP_LEN * NSA_HEAD_DIM, CMP_HIDDEN), (CMP_LEN * NSA_HEAD_DIM) ** -0.5)
    cmp_w2_k = nrm(ks[15], (DEPTH_2, CMP_HIDDEN, NSA_HEAD_DIM), CMP_HIDDEN ** -0.5)
    cmp_pe_v = nrm(ks[16], (DEPTH_2, CMP_LEN, NSA_HEAD_DIM), 0.1)
    cmp_w1_v = nrm(ks[17], (DEPTH_2, CMP_LEN * NSA_HEAD_DIM, CMP_HIDDEN), (CMP_LEN * NSA_HEAD_DIM) ** -0.5)
    cmp_w2_v = nrm(ks[18], (DEPTH_2, CMP_HIDDEN, NSA_HEAD_DIM), CMP_HIDDEN ** -0.5)
    nsa_norm_g = 1.0 + nrm(ks[19], (DEPTH_2, NSA_HEAD_DIM), 0.02)
    mix_w_out = nrm(ks[20], (DEPTH_2, MIX_WIDTH, D_MODEL), MIX_WIDTH ** -0.5)
    final_norm_g = 1.0 + nrm(ks[21], (D_MODEL,), 0.02)
    return {"x": x, "c": c, "positions": positions, "ada_w": ada_w, "ada_b": ada_b,
            "norm_g": norm_g, "ffn_w_in": ffn_w_in, "ffn_w_out": ffn_w_out,
            "mix_w_in": mix_w_in, "gdn_conv_w": gdn_conv_w, "gdn_a_log": gdn_a_log,
            "gdn_dt_bias": gdn_dt_bias, "gdn_norm_g": gdn_norm_g,
            "cmp_pe_k": cmp_pe_k, "cmp_w1_k": cmp_w1_k, "cmp_w2_k": cmp_w2_k,
            "cmp_pe_v": cmp_pe_v, "cmp_w1_v": cmp_w1_v, "cmp_w2_v": cmp_w2_v,
            "nsa_norm_g": nsa_norm_g, "mix_w_out": mix_w_out, "final_norm_g": final_norm_g}

def second_block(x, c, positions, ada_w, ada_b, norm_g, ffn_w_in, ffn_w_out, mix_w_in,
              gdn_conv_w, gdn_a_log, gdn_dt_bias, gdn_norm_g, cmp_pe_k, cmp_w1_k, cmp_w2_k,
              cmp_pe_v, cmp_w1_v, cmp_w2_v, nsa_norm_g, mix_w_out, final_norm_g):
    B, T, D = x.shape
    half = ROT_DIM // 2
    inv_freq = jnp.power(ROPE_THETA, -jnp.arange(half, dtype=jnp.float32) * (2.0 / ROT_DIM))
    ang = positions.astype(jnp.float32)[..., None] * inv_freq
    cos = jnp.cos(ang)[:, :, None, :]
    sin = jnp.sin(ang)[:, :, None, :]
    cond = jax.nn.silu(c.astype(jnp.float32))
    for l in range(DEPTH_2):
        mod = (cond @ ada_w[l].astype(jnp.float32) + ada_b[l].astype(jnp.float32)).reshape(B, 3, 3, D).astype(x.dtype)
        h = modulate(rms_norm_2(x, norm_g[l, 0]), mod[:, 0, 0], mod[:, 0, 1])
        x = x + 0.5 * mod[:, 0, 2][:, None, :] * swiglu(h, ffn_w_in[l, 0], ffn_w_out[l, 0])
        h = modulate(rms_norm_2(x, norm_g[l, 1]), mod[:, 1, 0], mod[:, 1, 1])
        y = token_mix(h, mix_w_in[l], gdn_conv_w[l], gdn_a_log[l], gdn_dt_bias[l], gdn_norm_g[l],
                      cmp_pe_k[l], cmp_w1_k[l], cmp_w2_k[l], cmp_pe_v[l], cmp_w1_v[l], cmp_w2_v[l],
                      nsa_norm_g[l], mix_w_out[l], cos, sin)
        x = x + mod[:, 1, 2][:, None, :] * y.astype(x.dtype)
        h = modulate(rms_norm_2(x, norm_g[l, 2]), mod[:, 2, 0], mod[:, 2, 1])
        x = x + 0.5 * mod[:, 2, 2][:, None, :] * swiglu(h, ffn_w_in[l, 1], ffn_w_out[l, 1])
    return rms_norm_2(x, final_norm_g)


def setup_inputs(seed=0):
    out = dict(first_inputs(seed))
    for name, value in second_inputs(seed + 1).items():
        if name != "x":
            out[name + "_2"] = value
    return out


def reference(
    x, norm1_g, w_in, ssd_conv_w, ssd_conv_b, dt_bias, a_log, d_skip, ssd_norm_g, w_ssd_proj,
    q_norm_g, k_norm_g, w_attn_proj, w_out, norm2_g, w_up, ffn_conv_w, ffn_conv_b, w_down, c_2,
    positions_2, ada_w_2, ada_b_2, norm_g_2, ffn_w_in_2, ffn_w_out_2, mix_w_in_2, gdn_conv_w_2,
    gdn_a_log_2, gdn_dt_bias_2, gdn_norm_g_2, cmp_pe_k_2, cmp_w1_k_2, cmp_w2_k_2, cmp_pe_v_2,
    cmp_w1_v_2, cmp_w2_v_2, nsa_norm_g_2, mix_w_out_2, final_norm_g_2,
):
    x = first_block(
        x, norm1_g, w_in, ssd_conv_w, ssd_conv_b, dt_bias, a_log, d_skip, ssd_norm_g,
        w_ssd_proj, q_norm_g, k_norm_g, w_attn_proj, w_out, norm2_g, w_up, ffn_conv_w,
        ffn_conv_b, w_down,
    )
    return second_block(
        x, c_2, positions_2, ada_w_2, ada_b_2, norm_g_2, ffn_w_in_2, ffn_w_out_2, mix_w_in_2,
        gdn_conv_w_2, gdn_a_log_2, gdn_dt_bias_2, gdn_norm_g_2, cmp_pe_k_2, cmp_w1_k_2,
        cmp_w2_k_2, cmp_pe_v_2, cmp_w1_v_2, cmp_w2_v_2, nsa_norm_g_2, mix_w_out_2,
        final_norm_g_2,
    )


_drawn_inputs = setup_inputs


def setup_inputs(seed=0):
    import zlib

    import numpy as np

    out = dict(_drawn_inputs(seed))
    spreads = {}
    factors = {'ssd_conv_b': 3.654,
     'q_norm_g': 8.0,
     'k_norm_g': 8.0,
     'ffn_conv_b': 4.199,
     'norm_g_2': 7.277,
     'gdn_norm_g_2': 8.0,
     'cmp_pe_k_2': 8.0,
     'cmp_pe_v_2': 21.067,
     'nsa_norm_g_2': 60.156,
     'final_norm_g_2': 8.103}
    for name, (base, spread) in spreads.items():
        noise = np.random.default_rng([zlib.crc32(name.encode()), seed]).standard_normal(out[name].shape)
        drawn = base * np.exp(spread * noise) if base else spread * noise
        out[name] = __import__('jax').numpy.asarray(drawn.astype(out[name].dtype))
    for name, factor in factors.items():
        out[name] = (out[name] * factor).astype(out[name].dtype)
    return out
```

```python
import concourse.bass as bass
from concourse import mybir
from contextlib import ExitStack, contextmanager
import numpy as np

F32 = mybir.dt.float32
F32R = mybir.dt.float32r
I32 = mybir.dt.int32
ALU = mybir.AluOpType
ACT = mybir.ActivationFunctionType
AX = mybir.AxisListType.X
P = 128
T = 512
D = 1024
KD = D // P
NB = T // P
UNIT = 2048
FF = 2816
NJ = FF // P
GROUPS = 8
LAYERS = 2
EPS = 1e-6
NEG = -1e30

MASKS = ("ident", "ones", "tri", "bd64", "tri64", "inv1", "inv2", "inv4", "inv8", "inv16", "inv32",
         "band", "causal", "mod4", "mod4c", "mod16", "mod16c", "swap", "cmp")
MI = {name: i for i, name in enumerate(MASKS)}

C1 = {}
C2 = {}


def _columns(table, spec):
    at = 0
    for name, n in spec:
        table[name] = at
        at += n
    return at


NC1 = _columns(C1, [("zero", 1), ("eps", 1), ("norm1", 8), ("conv_w", 128), ("conv_b", 32), ("dskip", 16),
                    ("ssd_norm", 16), ("qg", 1), ("kg", 1), ("norm2", 8), ("ffn_w", NJ * 6), ("ffn_b", NJ * 2),
                    ("cvec", 8), ("qks", 2), ("freq", 1), ("rots", 1), ("final", 8)])
NC2 = _columns(C2, [("norm", 24), ("adab", 72), ("conv_w", 48), ("gdn_norm", 1), ("pe", 64), ("w2k", 64),
                    ("w2v", 64)])
NR1 = 64
NR2 = 4 + 4 + 64

UR_DT, UR_SSD, UR_Z, UR_GSSD, UR_SPROJ = 1, 8, 4, 2, 4
UR_ATT, UR_APROJ, UR_OUT, UR_UP, UR_DOWN = 12, 1, 2, 11, 8
UR1 = UR_DT + UR_SSD + UR_Z + UR_GSSD + UR_SPROJ + UR_ATT + UR_APROJ + UR_OUT + UR_UP + UR_DOWN
UR_MIX = 9
UR2 = 2 * (UR_UP + UR_DOWN) + UR_MIX
NUR = UR1 + LAYERS * UR2
NADA = 36


class Kit:
    pass


class Pos:

    def __init__(self, K, eng, own):
        self.K, self.eng, self.own = K, eng, own
        self.v, self.tally = {}, {}

    def _add(self, name, k):
        self.v[name] = self.v.get(name, 0) + k
        self.tally[name] = self.tally.get(name, 0) + k
        return self.v[name]

    def next(self, name, k=1):
        return self._add(name, k)

    def value(self, name):
        return self.v.get(name, 0)

    def skip(self, name, k=1):
        self._add(name, k)

    def tick(self):
        self._add("own", 1)
        return 1

    def ticks(self):
        return self.v["own"]

    @contextmanager
    def loop(self, n):
        K = self.K
        self.eng.sem_inc(self.own, self.tick())
        key = K.next_loop(self)
        per = K.sizes.get(key, {})
        before, tally = dict(self.v), dict(self.tally)
        with self.eng.Fori(0, n) as i:
            for name in per:
                self.v[name] = before.get(name, 0) + i * per[name]
            yield i
        grown = {m: t - tally.get(m, 0) for m, t in self.tally.items() if t != tally.get(m, 0)}
        if K.dry:
            K.sizes[key] = grown
        assert K.dry or grown == per, (key, grown, per)
        for name, g in grown.items():
            self.v[name] = before.get(name, 0) + n * g
            self.tally[name] = tally.get(name, 0) + n * g


def sem_of(K, ctx):
    table = {}

    def sem(name):
        if name not in table:
            table[name] = ctx.enter_context(K.nc.semaphore(name))
        return table[name]
    return sem


def build(nc, a, plan, sizes=None):
    K = Kit()
    K.nc, K.a, K.dry, K.sizes = nc, a, sizes is None, {} if sizes is None else sizes
    loops = {}

    def next_loop(pos):
        name = pos.name
        loops[name] = loops.get(name, 0) + 1
        return name, loops[name]
    K.next_loop = next_loop
    with ExitStack() as ctx:
        K.sem = sem_of(K, ctx)
        memory(K, ctx)
        block = ctx.enter_context(nc.Block())

        @block.sync
        def _(sp):
            program_sync(K, sp, plan)

        @block.gpsimd
        def _(pool):
            program_pool(K, pool, plan)

        @block.tensor
        def _(pe):
            program(K, pe, "own_pe", PE_PARTS, plan)

        @block.scalar
        def _(act):
            program(K, act, "own_act", ACT_PARTS, plan)

        @block.vector
        def _(dve):
            program(K, dve, "own_dve", DVE_PARTS, plan)
    return K.sizes


def program(K, eng, own, parts, plan):
    pos = Pos(K, eng, K.sem(own))
    pos.name = own
    parts["start"](K, eng, pos)
    pos.layer = 0
    for part in plan[0]:
        parts[part](K, eng, pos)
    if plan[1]:
        with pos.loop(LAYERS) as layer:
            pos.layer = layer
            for part in plan[1]:
                parts[part](K, eng, pos)
    for part in plan[2]:
        parts[part](K, eng, pos)


def memory(K, ctx):
    nc = K.nc

    def at(name, where, shape, dt=F32):
        buffer = nc.alloc_sbuf_tensor_at(name, shape, dt, offset=where)
        end = where + -(-int(np.prod(shape[1:])) * 4 // 32) * 32
        K.top = max(K.top, end)
        return buffer, end
    K.top = 0
    KB = 1024
    K.x, o = at("x", -(-nc.sbuf_base // 32) * 32, [P, KD, T])
    K.h_hi, o = at("h_hi", o, [P, KD, T], F32R)
    K.h_lo, o = at("h_lo", o, [P, KD, T], F32R)
    K.w_raw, o = at("w_raw", o, [P, 2, UNIT])
    K.w_hi, o = at("w_hi", o, [P, 2, UNIT], F32R)
    K.w_lo, o = at("w_lo", o, [P, 2, UNIT], F32R)
    K.masks, o = at("masks", o, [P, len(MASKS), P])
    K.cols, o = at("cols", o, [P, NC1])
    K.cols2, o = at("cols2", o, [P, NC2])
    K.rows, o = at("rows", o, [P, NR1])
    K.rows2, o = at("rows2", o, [P, NR2])
    K.mods, o = at("mods", o, [P, 72])
    K.csilu, o = at("csilu", o, [P, 8])
    arena = K.arena = o
    K.n_sq, o = at("n_sq", arena, [P, 2, T])
    K.n_rstd, o = at("n_rstd", o, [P, T])
    K.n_t, o = at("n_t", o, [P, 2, T])
    K.ada_w, o = at("ada_w", arena + 16 * KB, [P, 2, UNIT])
    K.ada_acc, o = at("ada_acc", o, [P, 2, 256])
    K.act_hi, o = at("act_hi", arena, [P, NJ, T], F32R)
    K.act_lo, o = at("act_lo", o, [P, NJ, T], F32R)
    K.f_acc, o = at("f_acc", o, [P, 4, T])
    K.y, o = at("y", arena, [P, 16, T])
    K.y_lo, _ = at("y_lo", arena, [P, 16, T], F32R)
    K.y_hi, _ = at("y_hi", o, [P, 16, T], F32R)
    K.z_s, z = at("z_s", arena + 64 * KB, [P, 2, T])
    K.z_q, z = at("z_q", z, [P, 2, T])
    K.z_r, _ = at("z_r", z, [P, T])
    K.s_dt, o = at("s_dt", o, [P, NB, 32])
    K.s_a, o = at("s_a", o, [P, NB, 32])
    K.s_acs, o = at("s_acs", o, [P, NB, 32])
    K.s_dec, o = at("s_dec", o, [P, NB, 32])
    K.dt_s = nc.alloc_sbuf_tensor_at("dt_scratch", [P, 7, P], F32, offset=o)
    K.s_ag, o = at("s_ag", o, [P, NB, 4])
    K.s_xbc, o = at("s_xbc", o, [P, 4, T])
    K.s_btok, o = at("s_btok", o, [P, NB, P])
    K.s_cbt, o = at("s_cbt", o, [P, NB, P])
    K.s_X, o = at("s_X", o, [P, NB, 4, 64])
    K.s_X2, o = at("s_X2", o, [P, NB, 4, 64])
    K.s_eb, o = at("s_eb", o, [P, 4, T])
    K.s_m, o = at("s_m", o, [P, 4, T])
    K.s_ce, o = at("s_ce", o, [P, 4, T])
    K.s_st, o = at("s_st", o, [P, 3, 256])
    K.merged, _ = at("merged", arena + 64 * KB, [P, KD, T])
    K.mg_lo, _ = at("mg_lo", arena + 64 * KB, [P, KD, T], F32R)
    K.mg_hi, _ = at("mg_hi", arena, [P, KD, T], F32R)
    K.mg_t, _ = at("mg_t", arena + 32 * KB, [P, 2, T])
    K.a_qk, o = at("a_qk", arena, [P, 6, T])
    K.a_v, o = at("a_v", o, [P, NB, 3, P])
    K.a_sq, o = at("a_sq", o, [P, 2, T])
    K.a_rs, o = at("a_rs", o, [P, 2, T])
    K.a_p, o = at("a_p", o, [P, 1280])
    K.a_pt, o = at("a_pt", o, [P, 10, P])
    K.a_stat, o = at("a_stat", o, [P, 8])
    K.a_sig, _ = at("a_sig", arena + 44 * KB, [P, KD, T])
    K.a_y, o = at("a_y", arena + 80 * KB, [P, NB, T])
    K.a_yhi, o = at("a_yhi", arena + 16 * KB, [P, NB, T], F32R)
    K.a_ylo, o = at("a_ylo", o, [P, NB, T], F32R)
    mix_memory(K, at, arena, KB)
    assert K.top <= nc.sbuf_usable_end, K.top - nc.sbuf_usable_end
    K.g = [ctx.enter_context(nc.psum_tensor(f"g{i}", [P, T], F32)) for i in range(4)]
    K.p = [ctx.enter_context(nc.psum_tensor(f"p{i}", [P, T], F32)) for i in range(4)]
    K.mask = lambda name: K.masks[:, MI[name], :]
    K.col = lambda name, i=0, n=1: (K.cols[:, bass.ds(i + C1[name], n)] if not isinstance(i, int)
                                    else K.cols[:, C1[name] + i:C1[name] + i + n])
    K.col2 = lambda name, i=0, n=1: (K.cols2[:, bass.ds(i + C2[name], n)] if not isinstance(i, int)
                                     else K.cols2[:, C2[name] + i:C2[name] + i + n])


def idx(t, i):
    if isinstance(i, int):
        return t[:, i, :]
    return t[:, bass.ds(i, 1), :].rearrange("p a t -> p (a t)")



def program_sync(K, sp, plan):
    a = K.a
    consts = K.sem("consts_in")
    for dst, src in ((K.masks[:], a["masks"]), (K.cols[:], a["cols1"]), (K.x[:], a["x"]),
                     (K.rows[:], a["rows1"].broadcast_to([P, NR1]))):
        sp.dma_start(dst, src).then_inc(consts, 16)
    for s in range(2):
        sp.dma_start(K.w_raw[:, s], a["stream"][s]).then_inc(K.sem(f"raw_in{s}"), 16)
    with sp.Fori(1, plan_pairs(plan)) as r:
        for s in range(2):
            sp.wait_ge(K.sem("w_lo"), r * 2 + s - 1)
            sp.dma_start(K.w_raw[:, s], a["stream"][bass.ds(r * 2 + s, 1)].rearrange("a p c -> p (a c)")
                         ).then_inc(K.sem(f"raw_in{s}"), 16)
    sp.wait_ge(K.sem("result"), 1)
    sp.dma_start(a["out"], K.x[:]).then_inc(K.sem("out_done"), 16)
    sp.wait_ge(K.sem("out_done"), 16)


def program_pool(K, pool, plan):
    with pool.Fori(0, plan_pairs(plan)) as r:
        for s in range(2):
            pool.wait_ge(K.sem("w_hi"), r * 2 + s + 1)
            K.nc.gpsimd.tensor_tensor(K.w_lo[:, s], K.w_raw[:, s], K.w_hi[:, s].bitcast(F32), ALU.subtract
                                      ).then_inc(K.sem("w_lo"), 1)


def split_unit(K, act, pos, s):
    act.wait_ge(K.sem(f"raw_in{s}"), pos.next(f"raw_in{s}", 16))
    act.activation(K.w_hi[:, s], K.w_raw[:, s], ACT.Copy).then_inc(K.sem("w_hi"), 1)


def three_pass(K, out, w_hi, w_lo, h_hi, h_lo, start, stop):
    nc = K.nc
    nc.tensor.matmul(out, w_lo, h_hi, start=start, stop=False)
    nc.tensor.matmul(out, w_hi, h_lo, start=False, stop=False)
    return nc.tensor.matmul(out, w_hi, h_hi, start=False, stop=stop)


def gemm(K, pos, s, banks, hi, lo, width=256, ks=range(8), starts=True, ends=True, c0=0):
    for n, b in enumerate(banks):
        if starts:
            pos.eng.wait_ge(K.sem(f"g_free{b}"), pos.next(f"g_free{b}"))
        for i, k in enumerate(ks):
            w = slice(i * width + c0 + n * P, i * width + c0 + n * P + P)
            last = three_pass(K, K.g[b][:], K.w_hi[:, s, w], K.w_lo[:, s, w], hi[:, k, :], lo[:, k, :],
                              starts and i == 0, ends and i == len(ks) - 1)
        last.then_inc(K.sem("part"), 1)


def gemm_tok(K, pos, s, n, at=0, c0=0, free=True):
    for c in range(NB):
        if free:
            pos.eng.wait_ge(K.sem(f"g_free{c}"), pos.next(f"g_free{c}"))
        t = slice(c * P, c * P + P)
        for k in range(KD):
            w = slice(k * 256 + c0, k * 256 + c0 + n)
            last = three_pass(K, K.g[c][:, at:at + n], K.h_hi[:, k, t], K.h_lo[:, k, t],
                              K.w_hi[:, s, w], K.w_lo[:, s, w], k == 0, k == KD - 1)
        last.then_inc(K.sem("part"), 1)



def pe_start(K, pe, pos):
    pe.wait_ge(K.sem("consts_in"), 64)


def act_start(K, act, pos):
    act.wait_ge(K.sem("consts_in"), 64)
    split_unit(K, act, pos, 0)
    split_unit(K, act, pos, 1)


def dve_start(K, dve, pos):
    dve.wait_ge(K.sem("consts_in"), 64)
    for b in range(4):
        dve.sem_inc(K.sem(f"g_free{b}"), 1)
    dve.sem_inc(K.sem("x_ready"), 1)
    dve.sem_inc(K.sem("ada_free"), 1)
    dve.sem_inc(K.sem("ada_free"), 1)



def pe_norm(K, pe, pos):
    for k in range(KD):
        pe.wait_ge(K.sem("sq"), pos.next("sq"))
        K.nc.tensor.matmul(K.p[0][:], K.mask("ones"), K.n_sq[:, k % 2], start=k == 0, stop=k == KD - 1
            ).then_inc(K.sem("sq_used"), 1)
    pe.wait_ge(K.sem("h_lo"), pos.next("h_lo", KD))


def act_norm(K, act, pos, shift):
    act.wait_ge(K.sem("x_ready"), pos.next("x_ready"))
    for k in range(KD):
        if k >= 2:
            act.wait_ge(K.sem("sq_used"), pos.next("sq_used"))
        act.activation(K.n_sq[:, k % 2], K.x[:, k], ACT.Square).then_inc(K.sem("sq"), 1)
    act.wait_ge(K.sem("sq_used"), pos.next("sq_used", 2))
    act.activation(K.n_rstd[:], K.p[0][:], ACT.Sqrt, scale=1.0 / D, bias=K.col("eps")).then_inc(K.sem("n_std"), 1)
    for k in range(KD):
        act.wait_ge(K.sem("n_t"), pos.next("n_t"))
        act.activation(K.h_hi[:, k], K.n_t[:, k % 2], ACT.Identity, bias=shift(k)).then_inc(K.sem("h_hi"), 1)


def dve_norm(K, dve, pos, gain, shift):
    v = K.nc.vector
    dve.wait_ge(K.sem("n_std"), pos.next("n_std"))
    v.reciprocal(K.n_rstd[:], K.n_rstd[:]).then_inc(pos.own, pos.tick())
    dve.wait_ge(pos.own, pos.ticks())
    for k in range(KD + 1):
        if k < KD:
            v.scalar_tensor_tensor(K.n_t[:, k % 2], K.x[:, k], gain(k), K.n_rstd[:], ALU.mult, ALU.mult
                ).then_inc(pos.own, pos.tick())
            dve.wait_ge(pos.own, pos.ticks())
            dve.sem_inc(K.sem("n_t"), 1)
        if k:
            dve.wait_ge(K.sem("h_hi"), pos.next("h_hi"))
            v.scalar_tensor_tensor(K.h_lo[:, k - 1], K.n_t[:, (k - 1) % 2], shift(k - 1),
                                   K.h_hi[:, k - 1].bitcast(F32), ALU.add, ALU.subtract).then_inc(pos.own, pos.tick())
            dve.wait_ge(pos.own, pos.ticks())
            dve.sem_inc(K.sem("h_lo"), 1)


def norm_parts(name):
    gain, shift = (lambda K: lambda k: K.col(name, k)), (lambda K: lambda k: K.col("zero"))
    return (pe_norm, lambda K, e, p: act_norm(K, e, p, shift(K)),
            lambda K, e, p: dve_norm(K, e, p, gain(K), shift(K)))



def pe_dt(K, pe, pos):
    pe.wait_ge(K.sem("w_lo"), pos.next("w_lo"))
    gemm_tok(K, pos, 0, 32)
    pe.wait_ge(K.sem("w_lo"), pos.next("w_lo"))
    pe.wait_ge(K.sem("dt_a"), pos.next("dt_a"))
    K.nc.tensor.matmul(K.p[0][:, 0:P], K.mask("tri"), K.s_a[:].rearrange("p c h -> p (c h)"), start=True, stop=True)
    K.nc.tensor.matmul(K.p[1][:, 0:P], K.mask("ones"), K.s_a[:].rearrange("p c h -> p (c h)"),
                       start=True, stop=True).then_inc(K.sem("acs"), 1)
    pe.wait_ge(K.sem("dt_done"), pos.next("dt_done"))


def act_dt(K, act, pos):
    act.wait_ge(K.sem("part"), pos.next("part", 4))
    split_unit(K, act, pos, 0)
    act.wait_ge(K.sem("w_lo"), 2)
    split_unit(K, act, pos, 1)
    S = K.dt_s
    act.activation(S[:, 6, 0:32], K.rows[:, 32:64], ACT.Exp).then_inc(K.sem("dt_ea"), 1)
    act.wait_ge(K.sem("dt_n"), pos.next("dt_n"))
    act.activation(S[:, 2], S[:, 1], ACT.Exp).then_inc(K.sem("dt_e"), 1)
    act.wait_ge(K.sem("dt_u"), pos.next("dt_u"))
    act.activation(S[:, 5], S[:, 3], ACT.Ln).then_inc(K.sem("dt_l"), 1)
    act.wait_ge(K.sem("dt_d"), pos.next("dt_d"))
    act.activation(K.s_dec[:], K.s_dec[:], ACT.Exp).then_inc(K.sem("dt_x"), 1)


def softplus(K, pos, S, out):
    v = K.nc.vector
    v.scalar_tensor_tensor(S[1], S[0], -1.0, S[0], ALU.mult, ALU.min).then_inc(pos.own, pos.tick())
    pos.eng.wait_ge(pos.own, pos.ticks())
    pos.eng.sem_inc(K.sem("dt_n"), 1)
    pos.eng.wait_ge(K.sem("dt_e"), pos.next("dt_e"))
    v.tensor_scalar(S[3], S[2], 1.0, None, ALU.add).then_inc(pos.own, pos.tick())
    pos.eng.wait_ge(pos.own, pos.ticks())
    pos.eng.sem_inc(K.sem("dt_u"), 1)
    v.tensor_scalar(S[4], S[3], -1.0, None, ALU.add).then_inc(pos.own, pos.tick())
    pos.eng.wait_ge(pos.own, pos.ticks())
    v.tensor_tensor(S[4], S[2], S[4], ALU.subtract).then_inc(pos.own, pos.tick())
    pos.eng.wait_ge(pos.own, pos.ticks())
    pos.eng.wait_ge(K.sem("dt_l"), pos.next("dt_l"))
    v.reciprocal(S[3], S[3]).then_inc(pos.own, pos.tick())
    pos.eng.wait_ge(pos.own, pos.ticks())
    v.tensor_tensor(S[4], S[4], S[3], ALU.mult).then_inc(pos.own, pos.tick())
    pos.eng.wait_ge(pos.own, pos.ticks())
    v.tensor_tensor(S[5], S[5], S[4], ALU.add).then_inc(pos.own, pos.tick())
    pos.eng.wait_ge(pos.own, pos.ticks())
    v.scalar_tensor_tensor(out, S[0], 0.0, S[5], ALU.max, ALU.add).then_inc(pos.own, pos.tick())
    pos.eng.wait_ge(pos.own, pos.ticks())


def dve_dt(K, dve, pos):
    v = K.nc.vector
    for c in range(NB):
        dve.wait_ge(K.sem("part"), pos.next("part"))
        v.tensor_tensor(K.dt_s[:, 0, c * 32:c * 32 + 32], K.g[c][:, 0:32], K.rows[:, 0:32], ALU.add
            ).then_inc(pos.own, pos.tick())
        dve.wait_ge(pos.own, pos.ticks())
        dve.sem_inc(K.sem(f"g_free{c}"), 1)
    softplus(K, pos, [K.dt_s[:, i] for i in range(7)], K.s_dt[:].rearrange("p c h -> p (c h)"))
    dve.wait_ge(K.sem("dt_ea"), pos.next("dt_ea"))
    ea = K.dt_s[:, 6, 0:32].unsqueeze(1).broadcast_to([P, NB, 32])
    v.scalar_tensor_tensor(K.s_a[:], K.s_dt[:], -1.0, ea, ALU.mult, ALU.mult).then_inc(pos.own, pos.tick())
    dve.wait_ge(pos.own, pos.ticks())
    dve.sem_inc(K.sem("dt_a"), 1)
    dve.wait_ge(K.sem("acs"), pos.next("acs"))
    v.tensor_copy(K.s_acs[:].rearrange("p c h -> p (c h)"), K.p[0][:, 0:P]).then_inc(pos.own, pos.tick())
    dve.wait_ge(pos.own, pos.ticks())
    v.tensor_tensor(K.s_dec[:].rearrange("p c h -> p (c h)"), K.p[1][:, 0:P],
                    K.s_acs[:].rearrange("p c h -> p (c h)"), ALU.subtract).then_inc(pos.own, pos.tick())
    dve.wait_ge(pos.own, pos.ticks())
    dve.sem_inc(K.sem("dt_d"), 1)
    dve.wait_ge(K.sem("dt_x"), pos.next("dt_x"))
    dve.sem_inc(K.sem("dt_done"), 1)



def pe_ssd(K, pe, pos):
    t = K.nc.tensor
    with pos.loop(GROUPS):
        for s in range(2):
            pe.wait_ge(K.sem("w_lo"), pos.next("w_lo"))
            gemm(K, pos, s, (2 * s, 2 * s + 1), K.h_hi, K.h_lo)
        pe.wait_ge(K.sem("xbc"), pos.next("xbc", 4))
        for c in range(NB):
            for n in range(2):
                last = t.transpose(K.p[c // 2][:, (c % 2) * 256 + n * P:(c % 2) * 256 + n * P + P],
                                   K.s_xbc[:, n, c * P:c * P + P], K.mask("ident"))
        last.then_inc(K.sem("xs_t"), 1)
        for c in range(NB):
            last = t.transpose(K.p[2][:, c * P:c * P + P], K.s_xbc[:, 2, c * P:c * P + P], K.mask("ident"))
        last.then_inc(K.sem("b_t"), 1)
        for c in range(NB):
            last = t.matmul(K.p[3][:, c * P:c * P + P], K.s_xbc[:, 2, c * P:c * P + P], K.s_xbc[:, 3, c * P:c * P + P],
                            start=True, stop=True)
        last.then_inc(K.sem("cb"), 1)
        pe.wait_ge(K.sem("x_dt"), pos.next("x_dt"))
        pe.wait_ge(K.sem("b_tok"), pos.next("b_tok"))
        for h in range(4):
            for c in range(NB):
                last = t.matmul(K.p[h][:, c * P:c * P + P], K.s_ag[:, c, h:h + 1].broadcast_to([P, P]), K.mask("tri"),
                                start=True, stop=True)
            last.then_inc(K.sem("bc"), 1)
        pe.wait_ge(K.sem("mce"), pos.next("mce", 4))
        for c in range(3):
            last = t.matmul(K.p[c][:, 0:256], K.s_btok[:, c], K.s_X2[:, c].rearrange("p h d -> p (h d)"),
                            start=True, stop=True)
        last.then_inc(K.sem("st_p"), 1)
        pe.wait_ge(K.sem("st"), pos.next("st"))
        for n in range(2):
            for e in range(2):
                h = 2 * n + e
                for c in range(NB):
                    o = K.p[n][64 * e:64 * e + 64, c * P:c * P + P]
                    last = t.matmul(o, K.s_X[:, c, h, :], K.s_m[:, h, c * P:c * P + P], start=True, stop=c == 0)
                    if c:
                        last = t.matmul(o, K.s_st[:, c - 1, h * 64:h * 64 + 64], K.s_ce[:, h, c * P:c * P + P],
                                        start=False, stop=True)
            last.then_inc(K.sem("y_p"), 1)
        pe.wait_ge(K.sem("y_read"), pos.next("y_read"))


def act_ssd(K, act, pos):
    with pos.loop(GROUPS):
        for s in range(2):
            act.wait_ge(K.sem("part"), pos.next("part", 2))
            split_unit(K, act, pos, s)
        for n in range(4):
            act.wait_ge(K.sem("conv"), pos.next("conv"))
            act.activation(K.s_xbc[:, n], K.s_m[:, n], ACT.Silu).then_inc(K.sem("xbc"), 1)
        act.wait_ge(K.sem("b_t"), pos.next("b_t"))
        act.activation(K.s_btok[:].rearrange("p c n -> p (c n)"), K.p[2][:], ACT.Copy).then_inc(K.sem("b_tok"), 1)
        for h in range(4):
            act.wait_ge(K.sem("bc"), pos.next("bc"))
            act.activation(K.s_eb[:, h], K.p[h][:], ACT.Exp).then_inc(K.sem("eb"), 1)
        for h in range(4):
            act.wait_ge(K.sem("seg"), pos.next("seg"))
            act.activation(K.s_m[:, h], K.s_m[:, h], ACT.Exp).then_inc(K.sem("seg_x"), 1)


def conv(K, pos, out, src, w, b, taps):
    v = K.nc.vector
    v.tensor_scalar(out, src, w(taps - 1), b, ALU.mult, ALU.add).then_inc(pos.own, pos.tick())
    pos.eng.wait_ge(pos.own, pos.ticks())
    for d in range(1, taps):
        v.scalar_tensor_tensor(out[:, d:], src[:, 0:T - d], w(taps - 1 - d), out[:, d:], ALU.mult, ALU.add
            ).then_inc(pos.own, pos.tick())
        pos.eng.wait_ge(pos.own, pos.ticks())


def dve_ssd(K, dve, pos):
    v = K.nc.vector
    with pos.loop(GROUPS) as g:
        for n in range(4):
            dve.wait_ge(K.sem("part"), pos.next("part"))
            conv(K, pos, K.s_m[:, n], K.g[n][:], lambda i: K.col("conv_w", g * 16 + n * 4 + i),
                 K.col("conv_b", g * 4 + n), 4)
            dve.sem_inc(K.sem("conv"), 1)
            dve.sem_inc(K.sem(f"g_free{n}"), 1)
        heads = bass.ds(g * 4, 4)
        v.tensor_copy(K.s_ag[:], K.s_a[:, :, heads]).then_inc(pos.own, pos.tick())
        dve.wait_ge(pos.own, pos.ticks())
        dve.wait_ge(K.sem("xs_t"), pos.next("xs_t"))
        for c in range(2):
            v.tensor_tensor(K.s_X[:, 2 * c:2 * c + 2], K.p[c][:].rearrange("p (c h d) -> p c h d", c=2, h=4),
                            K.s_dt[:, 2 * c:2 * c + 2, heads].unsqueeze(3).broadcast_to([P, 2, 4, 64]), ALU.mult
                ).then_inc(pos.own, pos.tick())
            dve.wait_ge(pos.own, pos.ticks())
        v.tensor_tensor(K.s_X2[:], K.s_X[:], K.s_dec[:, :, heads].unsqueeze(3).broadcast_to([P, NB, 4, 64]),
                        ALU.mult).then_inc(pos.own, pos.tick())
        dve.wait_ge(K.sem("cb"), pos.next("cb"))
        v.tensor_tensor(K.s_cbt[:], K.p[3][:].rearrange("p (c l) -> p c l", c=NB),
                        K.mask("tri").unsqueeze(1).broadcast_to([P, NB, P]), ALU.mult).then_inc(pos.own, pos.tick())
        dve.wait_ge(pos.own, pos.ticks())
        dve.sem_inc(K.sem("x_dt"), 1)

        def scores(h):
            dve.wait_ge(K.sem("seg_x"), pos.next("seg_x"))
            v.tensor_tensor(K.s_m[:, h], K.s_m[:, h], K.s_cbt[:].rearrange("p c l -> p (c l)"), ALU.mult
                ).then_inc(pos.own, pos.tick())
            dve.wait_ge(pos.own, pos.ticks())
            dve.sem_inc(K.sem("mce"), 1)
        for h in range(4):
            dve.wait_ge(K.sem("eb"), pos.next("eb"))
            for c in range(NB):
                v.tensor_scalar(K.s_m[:, h, c * P:c * P + P], K.p[h][:, c * P:c * P + P],
                                K.s_acs[:, c, bass.ds(g * 4 + h, 1)], 0.0, ALU.subtract, ALU.min
                    ).then_inc(pos.own, pos.tick())
            dve.wait_ge(pos.own, pos.ticks())
            dve.sem_inc(K.sem("seg"), 1)
            v.tensor_tensor(K.s_ce[:, h], K.s_xbc[:, 3], K.s_eb[:, h], ALU.mult).then_inc(pos.own, pos.tick())
            if h:
                scores(h - 1)
        scores(3)
        dve.wait_ge(K.sem("st_p"), pos.next("st_p"))
        v.tensor_copy(K.s_st[:, 0], K.p[0][:, 0:256]).then_inc(pos.own, pos.tick())
        dve.wait_ge(pos.own, pos.ticks())
        for c in (1, 2):
            last = K.s_eb[:, :, c * P + P - 1:c * P + P].broadcast_to([P, 4, 64])
            v.tensor_tensor(K.s_st[:, c].rearrange("p (h d) -> p h d", h=4),
                            K.s_st[:, c - 1].rearrange("p (h d) -> p h d", h=4), last, ALU.mult
                ).then_inc(pos.own, pos.tick())
            dve.wait_ge(pos.own, pos.ticks())
            v.tensor_tensor(K.s_st[:, c], K.s_st[:, c], K.p[c][:, 0:256], ALU.add).then_inc(pos.own, pos.tick())
            dve.wait_ge(pos.own, pos.ticks())
        dve.sem_inc(K.sem("st"), 1)
        for n in range(2):
            dve.wait_ge(K.sem("y_p"), pos.next("y_p"))
            v.scalar_tensor_tensor(idx(K.y, g * 2 + n), K.s_xbc[:, n], K.col("dskip", g * 2 + n), K.p[n][:],
                                   ALU.mult, ALU.add).then_inc(pos.own, pos.tick())
            dve.wait_ge(pos.own, pos.ticks())
        dve.sem_inc(K.sem("y_read"), 1)



def pe_z(K, pe, pos):
    with pos.loop(4):
        for s in range(2):
            pe.wait_ge(K.sem("w_lo"), pos.next("w_lo"))
            gemm(K, pos, s, (2 * s, 2 * s + 1), K.h_hi, K.h_lo)
            for n in range(2):
                pe.wait_ge(K.sem("head_sq"), pos.next("head_sq"))
                last = K.nc.tensor.matmul(K.p[0][:], K.mask("ones"), K.z_q[:, n], start=n == 0, stop=n == 1)
            last.then_inc(K.sem("head_sum"), 1)
    pe.wait_ge(K.sem("y_lo"), pos.next("y_lo", 16))


def act_z(K, act, pos):
    with pos.loop(4) as i:
        for s in range(2):
            for n in range(2):
                act.wait_ge(K.sem("part"), pos.next("part"))
                act.activation(K.z_s[:, n], K.g[2 * s + n][:], ACT.Silu).then_inc(K.sem("z_s"), 1)
            split_unit(K, act, pos, s)
            for n in range(2):
                act.wait_ge(K.sem("z_y"), pos.next("z_y"))
                act.activation(K.z_q[:, n], idx(K.y, i * 4 + 2 * s + n), ACT.Square).then_inc(K.sem("head_sq"), 1)
            act.wait_ge(K.sem("head_sum"), pos.next("head_sum"))
            act.activation(K.z_r[:], K.p[0][:], ACT.Sqrt, scale=1.0 / 256, bias=K.col("eps")
                ).then_inc(K.sem("head_std"), 1)
            for n in range(2):
                act.wait_ge(K.sem("y_n"), pos.next("y_n"))
                act.activation(idx(K.y_hi, i * 4 + 2 * s + n), idx(K.y, i * 4 + 2 * s + n), ACT.Copy
                    ).then_inc(K.sem("y_hi"), 1)


def dve_z(K, dve, pos):
    v = K.nc.vector
    with pos.loop(4) as i:
        for s in range(2):
            for n in range(2):
                y = idx(K.y, i * 4 + 2 * s + n)
                pos.skip("part")
                dve.wait_ge(K.sem("z_s"), pos.next("z_s"))
                v.tensor_tensor(y, y, K.z_s[:, n], ALU.mult).then_inc(pos.own, pos.tick())
                dve.wait_ge(pos.own, pos.ticks())
                dve.sem_inc(K.sem(f"g_free{2 * s + n}"), 1)
                dve.sem_inc(K.sem("z_y"), 1)
            dve.wait_ge(K.sem("head_std"), pos.next("head_std"))
            v.reciprocal(K.z_r[:], K.z_r[:]).then_inc(pos.own, pos.tick())
            dve.wait_ge(pos.own, pos.ticks())
            for n in range(2):
                m = i * 4 + 2 * s + n
                v.scalar_tensor_tensor(idx(K.y, m), idx(K.y, m), K.col("ssd_norm", m), K.z_r[:], ALU.mult, ALU.mult
                    ).then_inc(pos.own, pos.tick())
                dve.wait_ge(pos.own, pos.ticks())
                dve.sem_inc(K.sem("y_n"), 1)
            for n in range(2):
                m = i * 4 + 2 * s + n
                dve.wait_ge(K.sem("y_hi"), pos.next("y_hi"))
                v.tensor_tensor(idx(K.y_lo, m), idx(K.y, m), idx(K.y_hi, m).bitcast(F32), ALU.subtract
                    ).then_inc(pos.own, pos.tick())
                dve.wait_ge(pos.own, pos.ticks())
                dve.sem_inc(K.sem("y_lo"), 1)



def pe_gssd(K, pe, pos):
    with pos.loop(2):
        for s in range(2):
            pe.wait_ge(K.sem("w_lo"), pos.next("w_lo"))
            gemm(K, pos, s, (2 * s, 2 * s + 1), K.h_hi, K.h_lo)
    with pos.loop(2):
        for b in range(4):
            pe.wait_ge(K.sem("w_lo"), pos.next("w_lo"))
            gemm(K, pos, b % 2, (b,), K.y_hi, K.y_lo, width=P, ks=range(16))


def act_gssd(K, act, pos):
    act.wait_ge(K.sem("y_lo"), pos.next("y_lo", 16))
    with pos.loop(2) as i:
        for s in range(2):
            for n in range(2):
                b = 2 * s + n
                act.wait_ge(K.sem("part"), pos.next("part"))
                act.activation(idx(K.merged, i * 4 + b), K.g[b][:], ACT.Sigmoid).then_inc(pos.own, pos.tick())
            split_unit(K, act, pos, s)
            act.wait_ge(pos.own, pos.ticks())
            act.sem_inc(K.sem(f"g_free{2 * s}"), 1)
            act.sem_inc(K.sem(f"g_free{2 * s + 1}"), 1)
            act.sem_inc(K.sem("sig"), 1)
    with pos.loop(2):
        for b in range(4):
            act.wait_ge(K.sem("part"), pos.next("part"))
            split_unit(K, act, pos, b % 2)


def dve_gssd(K, dve, pos):
    v = K.nc.vector
    pos.skip("part", 8)
    dve.wait_ge(K.sem("sig"), pos.next("sig", 4))
    with pos.loop(2) as i:
        for b in range(4):
            dve.wait_ge(K.sem("part"), pos.next("part"))
            m = idx(K.merged, i * 4 + b)
            v.tensor_tensor(m, m, K.g[b][:], ALU.mult).then_inc(K.sem(f"g_free{b}"), 1)



def att_tiles(qb):
    t = [(0, qb - 1, "band")] if qb else []
    t.append((0, qb, "causal"))
    for g, m in ((1, "mod4"), (2, "mod16")):
        t += [(g, kb, m if kb < qb else m + "c") for kb in range(qb + 1)]
    return t


def pe_att(K, pe, pos):
    t = K.nc.tensor
    with pos.loop(4):
        for u in range(3):
            pe.wait_ge(K.sem("w_lo"), pos.next("w_lo"))
            b = 2 * (u % 2)
            gemm(K, pos, u % 2, (b, b + 1), K.h_hi, K.h_lo)
            if u:
                pe.wait_ge(K.sem("a_norm"), pos.next("a_norm", 2))
            for n in range(2):
                pe.wait_ge(K.sem("head_sq"), pos.next("head_sq"))
                t.matmul(K.p[n][:], K.mask("bd64"), K.a_sq[:, n], start=True, stop=True
                    ).then_inc(K.sem("head_sum"), 1)
        pe.wait_ge(K.sem("w_lo"), pos.next("w_lo"))
        gemm_tok(K, pos, 1, 256)
        pe.wait_ge(K.sem("w_lo"), pos.next("w_lo"))
        gemm_tok(K, pos, 0, P, at=256, free=False)
        gemm(K, pos, 0, (0,), K.h_hi, K.h_lo, c0=P)
        pe.wait_ge(K.sem("w_lo"), pos.next("w_lo"))
        gemm(K, pos, 1, (1,), K.h_hi, K.h_lo)
        pe.wait_ge(K.sem("a_vin"), pos.next("a_vin", 4))
        pe.wait_ge(K.sem("a_norm"), pos.next("a_norm", 2))
        for e in range(2):
            r = slice(64 * e, 64 * e + 64)
            for qb in range(NB):
                for g in range(3):
                    k0 = max(qb - 1, 0) * P if g == 0 else 0
                    n = (qb + 1) * P - k0
                    last = t.matmul(K.p[g][:, 0:n], K.a_qk[r, 2 * g, qb * P:qb * P + P], K.a_qk[r, 2 * g + 1, k0:k0 + n],
                                    start=True, stop=True)
                last.then_inc(K.sem("scores"), 1)
                tiles = att_tiles(qb)
                pe.wait_ge(K.sem("a_pe"), pos.next("a_pe"))
                for n in range(len(tiles)):
                    last = t.transpose(K.p[(3, 0, 1)[n // 4]][:, (n % 4) * P:(n % 4) * P + P], K.a_p[:, n * P:n * P + P],
                                       K.mask("ident"))
                    if n % 4 == 3 or n == len(tiles) - 1:
                        last.then_inc(K.sem("probs_t"), 1)
                for n, (g, kb, _) in enumerate(tiles):
                    if n % 4 == 0:
                        pe.wait_ge(K.sem("probs_t_read"), pos.next("probs_t_read"))
                    last = t.matmul(K.p[2][:, 0:64], K.a_pt[:, n], K.a_v[:, kb, g, r], start=n == 0,
                                    stop=n == len(tiles) - 1)
                last.then_inc(K.sem("a_pv"), 1)
                pe.wait_ge(K.sem("a_out"), pos.next("a_out"))


def act_att(K, act, pos):
    with pos.loop(4) as j:
        for u in range(3):
            b = 2 * (u % 2)
            for n in range(2):
                act.wait_ge(K.sem("part"), pos.next("part"))
                act.activation(K.a_sq[:, n], K.g[b + n][:], ACT.Square).then_inc(K.sem("head_sq"), 1)
            split_unit(K, act, pos, u % 2)
            for n in range(2):
                act.wait_ge(K.sem("head_sum"), pos.next("head_sum"))
                act.activation(K.a_rs[:, n], K.p[n][:], ACT.Sqrt, scale=1.0 / 64, bias=K.col("eps")
                    ).then_inc(K.sem("head_std"), 1)
        act.wait_ge(K.sem("part"), pos.next("part", 4))
        split_unit(K, act, pos, 1)
        act.wait_ge(K.sem("part"), pos.next("part", 5))
        split_unit(K, act, pos, 0)
        act.activation(idx(K.a_sig, j * 2), K.g[0][:], ACT.Sigmoid).then_inc(pos.own, pos.tick())
        act.wait_ge(pos.own, pos.ticks())
        act.sem_inc(K.sem("g_free0"), 1)
        act.wait_ge(K.sem("part"), pos.next("part"))
        split_unit(K, act, pos, 1)
        act.activation(idx(K.a_sig, j * 2 + 1), K.g[1][:], ACT.Sigmoid).then_inc(pos.own, pos.tick())
        act.wait_ge(pos.own, pos.ticks())
        act.sem_inc(K.sem("g_free1"), 1)
        for e in range(2):
            for qb in range(NB):
                n = len(att_tiles(qb))
                act.wait_ge(K.sem("row_max"), pos.next("row_max"))
                act.activation(K.a_p[:, 0:n * P], K.a_p[:, 0:n * P], ACT.Exp, scale=0.125, bias=K.a_stat[:, 1:2],
                               accum_out=K.a_stat[:, 2:3]).then_inc(K.sem("a_pe"), 1)
                for n4 in range(0, n, 4):
                    act.wait_ge(K.sem("probs_t"), pos.next("probs_t"))
                    w = min(4, n - n4) * P
                    act.activation(K.a_pt[:, n4:n4 + w // P].rearrange("p a b -> p (a b)"),
                                   K.p[(3, 0, 1)[n4 // 4]][:, 0:w], ACT.Copy).then_inc(K.sem("probs_t_read"), 1)


def dve_att(K, dve, pos):
    v = K.nc.vector
    with pos.loop(4) as j:
        for u in range(3):
            b = 2 * (u % 2)
            for n in range(2):
                pos.skip("part")
                dve.wait_ge(K.sem("head_std"), pos.next("head_std"))
                v.reciprocal(K.a_rs[:, n], K.a_rs[:, n]).then_inc(pos.own, pos.tick())
                dve.wait_ge(pos.own, pos.ticks())
                v.scalar_tensor_tensor(K.a_qk[:, 2 * u + n], K.g[b + n][:], K.col("kg" if n else "qg"),
                                       K.a_rs[:, n], ALU.mult, ALU.mult).then_inc(pos.own, pos.tick())
                dve.wait_ge(pos.own, pos.ticks())
                dve.sem_inc(K.sem(f"g_free{b + n}"), 1)
                dve.sem_inc(K.sem("a_norm"), 1)
        pos.skip("part", 4)
        for c in range(NB):
            dve.wait_ge(K.sem("part"), pos.next("part"))
            v.tensor_copy(K.a_v[:, c].rearrange("p g d -> p (g d)"), K.g[c][:, 0:3 * P]).then_inc(pos.own, pos.tick())
            dve.wait_ge(pos.own, pos.ticks())
            dve.sem_inc(K.sem(f"g_free{c}"), 1)
            dve.sem_inc(K.sem("a_vin"), 1)
        pos.skip("part", 2)
        for e in range(2):
            for qb in range(NB):
                tiles = att_tiles(qb)
                dve.wait_ge(K.sem("scores"), pos.next("scores"))
                at = 0
                for g in range(3):
                    mine = [x for x in tiles if x[0] == g]
                    if g and qb:
                        v.tensor_tensor(K.a_p[:, at:at + qb * P].rearrange("p (a b) -> p a b", b=P),
                                        K.p[g][:, 0:qb * P].rearrange("p (a b) -> p a b", b=P),
                                        K.mask(mine[0][2]).unsqueeze(1).broadcast_to([P, qb, P]), ALU.add
                            ).then_inc(pos.own, pos.tick())
                    m0 = MI[mine[0][2]] if g == 0 else MI[mine[-1][2]]
                    k = len(mine) if g == 0 else 1
                    o = (len(mine) - k) * P
                    v.tensor_tensor(K.a_p[:, at + o:at + o + k * P], K.p[g][:, o:o + k * P],
                                    K.masks[:, m0:m0 + k].rearrange("p a b -> p (a b)"), ALU.add
                        ).then_inc(pos.own, pos.tick())
                    at += len(mine) * P
                dve.wait_ge(pos.own, pos.ticks())
                v.reduce_max(K.a_stat[:, 0:1], K.a_p[:, 0:at], AX).then_inc(pos.own, pos.tick())
                dve.wait_ge(pos.own, pos.ticks())
                v.tensor_scalar(K.a_stat[:, 1:2], K.a_stat[:, 0:1], -0.125, None, ALU.mult
                    ).then_inc(pos.own, pos.tick())
                dve.wait_ge(pos.own, pos.ticks())
                dve.sem_inc(K.sem("row_max"), 1)
                dve.wait_ge(K.sem("a_pv"), pos.next("a_pv"))
                v.reciprocal(K.a_stat[:, 3:4], K.a_stat[:, 2:3]).then_inc(pos.own, pos.tick())
                dve.wait_ge(pos.own, pos.ticks())
                v.tensor_scalar(K.a_y[:, qb, bass.ds(j * P + 64 * e, 64)], K.p[2][:, 0:64], K.a_stat[:, 3:4], None,
                                ALU.mult).then_inc(pos.own, pos.tick())
                dve.wait_ge(pos.own, pos.ticks())
                dve.sem_inc(K.sem("a_out"), 1)



def pe_aproj(K, pe, pos):
    for f in range(4):
        for qb in range(NB):
            last = K.nc.tensor.transpose(K.p[f][:, qb * P:qb * P + P], K.a_y[:, qb, f * P:f * P + P], K.mask("ident"))
        last.then_inc(K.sem("yt"), 1)
    pe.wait_ge(K.sem("yt_lo"), pos.next("yt_lo", 4))
    for s in range(2):
        pe.wait_ge(K.sem("w_lo"), pos.next("w_lo"))
        gemm(K, pos, s, (0, 1, 2, 3), K.a_yhi, K.a_ylo, width=512, ks=range(4))


def act_aproj(K, act, pos):
    for f in range(4):
        act.wait_ge(K.sem("yt"), pos.next("yt"))
        act.activation(K.a_yhi[:, f], K.p[f][:], ACT.Copy).then_inc(K.sem("yt_hi"), 1)
    for s in range(2):
        act.wait_ge(K.sem("part"), pos.next("part", 4))
        split_unit(K, act, pos, s)
        for b in range(4):
            act.wait_ge(K.sem("mg"), pos.next("mg"))
            act.activation(K.mg_hi[:, 4 * s + b], K.merged[:, 4 * s + b], ACT.Copy).then_inc(K.sem("mg_hi"), 1)


def dve_aproj(K, dve, pos):
    v = K.nc.vector
    for f in range(4):
        dve.wait_ge(K.sem("yt_hi"), pos.next("yt_hi"))
        v.tensor_tensor(K.a_ylo[:, f], K.p[f][:], K.a_yhi[:, f].bitcast(F32), ALU.subtract
            ).then_inc(K.sem("yt_lo"), 1)
    for s in range(2):
        for b in range(4):
            m = 4 * s + b
            dve.wait_ge(K.sem("part"), pos.next("part"))
            v.tensor_tensor(K.mg_t[:, b % 2], K.g[b][:], K.a_sig[:, m], ALU.mult).then_inc(pos.own, pos.tick())
            dve.wait_ge(pos.own, pos.ticks())
            dve.sem_inc(K.sem(f"g_free{b}"), 1)
            v.tensor_tensor(K.merged[:, m], K.merged[:, m], K.mg_t[:, b % 2], ALU.add).then_inc(pos.own, pos.tick())
            dve.wait_ge(pos.own, pos.ticks())
            dve.sem_inc(K.sem("mg"), 1)
            dve.wait_ge(K.sem("mg_hi"), pos.next("mg_hi"))
            v.tensor_tensor(K.mg_lo[:, m], K.merged[:, m], K.mg_hi[:, m].bitcast(F32), ALU.subtract
                ).then_inc(pos.own, pos.tick())
            dve.wait_ge(pos.own, pos.ticks())
            dve.sem_inc(K.sem("mg_lo"), 1)



def pe_out(K, pe, pos):
    pe.wait_ge(K.sem("mg_lo"), pos.next("mg_lo", KD))
    with pos.loop(2):
        for s in range(2):
            pe.wait_ge(K.sem("w_lo"), pos.next("w_lo"))
            gemm(K, pos, s, (2 * s, 2 * s + 1), K.mg_hi, K.mg_lo)


def act_out(K, act, pos):
    with pos.loop(2):
        for s in range(2):
            act.wait_ge(K.sem("part"), pos.next("part", 2))
            split_unit(K, act, pos, s)


def add_to_x(K, pos, m, b, gate):
    v = K.nc.vector
    x = idx(K.x, m)
    if gate is None:
        v.tensor_tensor(x, x, K.g[b][:], ALU.add).then_inc(K.sem(f"g_free{b}"), 1)
    else:
        v.scalar_tensor_tensor(x, K.g[b][:], gate(m), x, ALU.mult, ALU.add).then_inc(K.sem(f"g_free{b}"), 1)


def dve_out(K, dve, pos, gate=None):
    with pos.loop(2) as i:
        for b in range(4):
            dve.wait_ge(K.sem("part"), pos.next("part"))
            add_to_x(K, pos, i * 4 + b, b, gate)
    x_done(K, pos)


def x_done(K, pos):
    K.nc.vector.tensor_copy(K.x[:, 0, 0:1], K.x[:, 0, 0:1]).then_inc(pos.own, pos.tick())
    pos.eng.wait_ge(pos.own, pos.ticks())
    pos.eng.sem_inc(K.sem("x_ready"), 1)



def pe_ffn(K, pe, pos):
    with pos.loop(UR_UP):
        for s in range(2):
            pe.wait_ge(K.sem("w_lo"), pos.next("w_lo"))
            gemm(K, pos, s, (2 * s, 2 * s + 1), K.h_hi, K.h_lo)
    pe.wait_ge(K.sem("act_lo"), pos.next("act_lo", NJ))
    with pos.loop(2):
        for u in range(8):
            pe.wait_ge(K.sem("w_lo"), pos.next("w_lo"))
            gemm(K, pos, u % 2, (u // 2,), K.act_hi, K.act_lo, width=P, ks=range(11 * (u % 2), 11 * (u % 2) + 11),
                 starts=u % 2 == 0, ends=u % 2 == 1)


def act_ffn(K, act, pos, conv):
    with pos.loop(UR_UP) as i:
        for s in range(2):
            acc = K.f_acc[:, 2 * s], K.f_acc[:, 2 * s + 1]
            if conv:
                act.wait_ge(K.sem("part"), pos.next("part", 2))
                split_unit(K, act, pos, s)
                act.wait_ge(K.sem("f_conv"), pos.next("f_conv"))
                act.activation(acc[0], acc[0], ACT.Silu).then_inc(K.sem("f_s"), 1)
            else:
                act.wait_ge(K.sem("part"), pos.next("part"))
                act.activation(acc[0], K.g[2 * s][:], ACT.Silu).then_inc(pos.own, pos.tick())
                act.wait_ge(pos.own, pos.ticks())
                act.sem_inc(K.sem(f"g_free{2 * s}"), 1)
                act.sem_inc(K.sem("f_s"), 1)
                act.wait_ge(K.sem("part"), pos.next("part"))
                split_unit(K, act, pos, s)
            act.wait_ge(K.sem("f_u"), pos.next("f_u"))
            act.activation(idx(K.act_hi, i * 2 + s), acc[1], ACT.Copy).then_inc(K.sem("act_hi"), 1)
    with pos.loop(2):
        for u in range(8):
            act.wait_ge(K.sem("part"), pos.next("part"))
            split_unit(K, act, pos, u % 2)


def dve_ffn(K, dve, pos, with_conv, gate):
    v = K.nc.vector
    with pos.loop(UR_UP) as i:
        for s in range(2):
            acc = K.f_acc[:, 2 * s], K.f_acc[:, 2 * s + 1]
            if with_conv:
                for n in range(2):
                    dve.wait_ge(K.sem("part"), pos.next("part"))
                    conv(K, pos, acc[n], K.g[2 * s + n][:], lambda q: K.col("ffn_w", i * 12 + s * 6 + n * 3 + q),
                         K.col("ffn_b", i * 4 + 2 * s + n), 3)
                    dve.sem_inc(K.sem(f"g_free{2 * s + n}"), 1)
                    if n == 0:
                        dve.sem_inc(K.sem("f_conv"), 1)
                dve.wait_ge(K.sem("f_s"), pos.next("f_s"))
                v.tensor_tensor(acc[1], acc[0], acc[1], ALU.mult).then_inc(pos.own, pos.tick())
                dve.wait_ge(pos.own, pos.ticks())
                dve.sem_inc(K.sem("f_u"), 1)
            else:
                dve.wait_ge(K.sem("part"), pos.next("part", 2))
                dve.wait_ge(K.sem("f_s"), pos.next("f_s"))
                v.tensor_tensor(acc[1], acc[0], K.g[2 * s + 1][:], ALU.mult).then_inc(pos.own, pos.tick())
                dve.wait_ge(pos.own, pos.ticks())
                dve.sem_inc(K.sem(f"g_free{2 * s + 1}"), 1)
                dve.sem_inc(K.sem("f_u"), 1)
            dve.wait_ge(K.sem("act_hi"), pos.next("act_hi"))
            v.tensor_tensor(idx(K.act_lo, i * 2 + s), acc[1], idx(K.act_hi, i * 2 + s).bitcast(F32),
                           ALU.subtract).then_inc(pos.own, pos.tick())
            dve.wait_ge(pos.own, pos.ticks())
            dve.sem_inc(K.sem("act_lo"), 1)
    with pos.loop(2) as i:
        for b in range(4):
            pos.skip("part")
            dve.wait_ge(K.sem("part"), pos.next("part"))
            add_to_x(K, pos, i * 4 + b, b, gate)
    x_done(K, pos)



def pe_final(K, pe, pos):
    for k in range(KD):
        pe.wait_ge(K.sem("sq"), pos.next("sq"))
        K.nc.tensor.matmul(K.p[0][:], K.mask("ones"), K.n_sq[:, k % 2], start=k == 0, stop=k == KD - 1
            ).then_inc(K.sem("sq_used"), 1)


def act_final(K, act, pos):
    act.wait_ge(K.sem("x_ready"), pos.next("x_ready"))
    for k in range(KD):
        if k >= 2:
            act.wait_ge(K.sem("sq_used"), pos.next("sq_used"))
        act.activation(K.n_sq[:, k % 2], K.x[:, k], ACT.Square).then_inc(K.sem("sq"), 1)
    act.wait_ge(K.sem("sq_used"), pos.next("sq_used", 2))
    act.activation(K.n_rstd[:], K.p[0][:], ACT.Sqrt, scale=1.0 / D, bias=K.col("eps")).then_inc(K.sem("n_std"), 1)


def dve_final(K, dve, pos):
    v = K.nc.vector
    dve.wait_ge(K.sem("n_std"), pos.next("n_std"))
    v.reciprocal(K.n_rstd[:], K.n_rstd[:]).then_inc(pos.own, pos.tick())
    dve.wait_ge(pos.own, pos.ticks())
    for k in range(KD):
        v.scalar_tensor_tensor(K.x[:, k], K.x[:, k], K.col("final", k), K.n_rstd[:], ALU.mult, ALU.mult
            ).then_inc(pos.own, pos.tick())
    dve.wait_ge(pos.own, pos.ticks())
    dve.sem_inc(K.sem("result"), 1)





def pe_ada(K, pe, pos):
    with pos.loop(NADA // 2) as i:
        for s in range(2):
            pe.wait_ge(K.sem("ada_acc"), pos.next("ada_acc"))
            for n in range(2):
                last = K.nc.tensor.matmul(K.p[0][:, bass.ds(i * 4 + 2 * s + n, 1)], K.ada_acc[:, s, n * P:n * P + P],
                                          K.mask("ones")[:, 0:1], start=True, stop=True)
            last.then_inc(K.sem("ada_mm"), 1)
    pe.wait_ge(K.sem("mods"), pos.next("mods"))
    pe.wait_ge(K.sem("cols2_in"), pos.next("cols2_in", 32))


def act_ada(K, act, pos):
    act.wait_ge(K.sem("x_ready"), pos.value("x_ready") + 1)
    act.activation(K.csilu[:], K.col("cvec", 0, 8), ACT.Silu).then_inc(pos.own, pos.tick())
    act.wait_ge(pos.own, pos.ticks())
    act.sem_inc(K.sem("cond"), 1)
    act.dma_start(K.cols2[:], K.a["cols2"][ds1(pos.layer)].rearrange("a p c -> p (a c)")).then_inc(K.sem("cols2_in"), 16)
    act.dma_start(K.rows2[:], K.a["rows2"][ds1(pos.layer)].broadcast_to([P, NR2])).then_inc(K.sem("cols2_in"), 16)
    with pos.loop(NADA // 2) as i:
        for s in range(2):
            act.wait_ge(K.sem("ada_free"), pos.next("ada_free"))
            act.dma_start(K.ada_w[:, s], K.a["ada"][bass.ds(pos.layer * NADA + i * 2 + s, 1)].rearrange("a p c -> p (a c)")
                          ).then_inc(K.sem(f"ada_in{s}"), 16)
    act.wait_ge(K.sem("mods"), pos.next("mods"))
    act.wait_ge(K.sem("cols2_in"), pos.next("cols2_in", 32))


def dve_ada(K, dve, pos):
    v = K.nc.vector
    dve.wait_ge(K.sem("cond"), pos.next("cond"))
    dve.sem_inc(K.sem("ada_mm"), 1)
    dve.sem_inc(K.sem("ada_mm"), 1)
    with pos.loop(NADA // 2):
        for s in range(2):
            dve.wait_ge(K.sem(f"ada_in{s}"), pos.next(f"ada_in{s}", 16))
            dve.wait_ge(K.sem("ada_mm"), pos.next("ada_mm"))
            acc = K.ada_acc[:, s]
            v.tensor_scalar(acc, K.ada_w[:, s, 0:256], K.csilu[:, 0:1], None, ALU.mult).then_inc(pos.own, pos.tick())
            dve.wait_ge(pos.own, pos.ticks())
            for k in range(1, KD):
                v.scalar_tensor_tensor(acc, K.ada_w[:, s, k * 256:k * 256 + 256], K.csilu[:, k:k + 1], acc,
                                       ALU.mult, ALU.add).then_inc(pos.own, pos.tick())
                dve.wait_ge(pos.own, pos.ticks())
            dve.sem_inc(K.sem("ada_acc"), 1)
            dve.sem_inc(K.sem("ada_free"), 1)
    dve.wait_ge(K.sem("ada_mm"), pos.next("ada_mm", 2))
    dve.wait_ge(K.sem("cols2_in"), pos.next("cols2_in", 32))
    m = K.mods
    v.tensor_tensor(m[:], K.p[0][:, 0:72], K.col2("adab", 0, 72), ALU.add).then_inc(pos.own, pos.tick())
    dve.wait_ge(pos.own, pos.ticks())
    for i in range(3):
        v.scalar_tensor_tensor(m[:, 24 * i + 8:24 * i + 16], m[:, 24 * i + 8:24 * i + 16], 1.0,
                               K.col2("norm", 8 * i, 8), ALU.add, ALU.mult).then_inc(pos.own, pos.tick())
        dve.wait_ge(pos.own, pos.ticks())
        if i != 1:
            v.tensor_scalar(m[:, 24 * i + 16:24 * i + 24], m[:, 24 * i + 16:24 * i + 24], 0.5, None, ALU.mult
                ).then_inc(pos.own, pos.tick())
            dve.wait_ge(pos.own, pos.ticks())
    dve.sem_inc(K.sem("mods"), 1)


def ds1(i):
    return bass.ds(i, 1)


def mod_norm_parts(i):
    def shift(K):
        return lambda k: K.mods[:, 24 * i + k:24 * i + k + 1]

    def gain(K):
        return lambda k: K.mods[:, 24 * i + 8 + k:24 * i + 9 + k]
    return (pe_norm, lambda K, e, p: act_norm(K, e, p, shift(K)),
            lambda K, e, p: dve_norm(K, e, p, gain(K), shift(K)))


def gate_of(K, i):
    def gate(m):
        return K.mods[:, bass.ds(m + 24 * i + 16, 1)]
    return gate



def mix_memory(K, at, arena, KB):
    K.m_yhi, _ = at("m_yhi", arena, [P, 8, T], F32R)
    K.m_ylo, _ = at("m_ylo", arena + 16 * KB, [P, 8, T], F32R)
    K.m_U, _ = at("m_U", arena, [P, 4, T])
    K.m_at, _ = at("m_at", arena + 8 * KB, [P, 4, T])
    K.m_nw, _ = at("m_nw", arena + 16 * KB, [P, 4, T])
    K.m_kbe, _ = at("m_kbe", arena + 24 * KB, [P, 4, T])
    K.m_v, o = at("m_v", arena + 32 * KB, [P, NB, 256])
    K.m_bag, o = at("m_bag", o, [P, NB, 32])
    K.m_sig, o = at("m_sig", o, [P, NB, 32])
    K.m_gl, o = at("m_gl", o, [P, NB, 4])
    K.m_gc, o = at("m_gc", o, [P, NB, 4])
    K.m_dl, o = at("m_dl", o, [P, NB, 4])
    K.m_be, o = at("m_be", o, [P, NB, 4])
    K.m_el, o = at("m_el", o, [P, 4, 8])
    K.m_ea, o = at("m_ea", o, [P, 4])
    assert o <= arena + 38 * KB
    K.m_qk, _ = at("m_qk", arena + 38 * KB, [P, 8, T])
    K.m_vf, _ = at("m_vf", arena + 54 * KB, [P, 4, T])
    K.m_o, _ = at("m_o", arena + 54 * KB, [P, 4, T])
    K.m_z, _ = at("m_z", arena + 62 * KB, [P, 4, T])
    K.m_vb, _ = at("m_vb", arena + 70 * KB, [P, 4, T])
    K.m_kd, _ = at("m_kd", arena + 78 * KB, [P, 4, T])
    o = arena + 86 * KB
    K.m_sq, _ = at("m_sq", o, [P, 2, T])
    K.m_rs, _ = at("m_rs", o + 4 * KB, [P, 2, T])
    K.m_sp, _ = at("m_sp", o + 8 * KB, [P, 7, 16])
    K.t_kb, _ = at("t_kb", o, [P, T])
    K.t_y, _ = at("t_y", o, [P, T])
    K.t_eb, _ = at("t_eb", o + 2 * KB, [P, T])
    K.t_vn, _ = at("t_vn", o + 2 * KB, [P, 4, P])
    K.t_d, _ = at("t_d", o + 4 * KB, [P, T])
    K.t_m, _ = at("t_m", o + 4 * KB, [P, T])
    K.t_l, _ = at("t_l", o + 6 * KB, [P, T])
    K.t_T, _ = at("t_T", o + 8 * KB, [P, T])
    K.m_S, _ = at("m_S", o + 10 * KB, [P, 4, P])
    K.n_q, _ = at("n_q", arena + 38 * KB, [P, 4, T])
    K.n_k, _ = at("n_k", arena + 46 * KB, [P, 4, T])
    K.n_cos, _ = at("n_cos", arena + 54 * KB, [P, T])
    K.n_sin, _ = at("n_sin", arena + 56 * KB, [P, T])
    K.n_w1, _ = at("n_w1", arena + 58 * KB, [P, 2, 32, P])
    K.n_blk, _ = at("n_blk", arena + 90 * KB, [P, 32, 32])
    K.n_pos, _ = at("n_pos", arena + 94 * KB, [P, T], I32)
    K.n_raw, _ = at("n_raw", arena + 94 * KB, [P, T])
    K.n_hid, o = at("n_hid", arena + 96 * KB, [P, 2, 32])
    K.n_kc, o = at("n_kc", o, [P, 32])
    K.n_vc, o = at("n_vc", o, [P, 2, 64])
    K.n_stat, o = at("n_stat", o, [P, 16])
    K.n_tmp, o = at("n_tmp", arena + 90 * KB, [P, T])
    K.n_p, o = at("n_p", arena + 58 * KB, [P, 32 + 2 * T])
    K.n_pt, o = at("n_pt", o, [P, 9, P])
    K.n_qs, o = at("n_qs", o, [P, T])
    K.n_y, o = at("n_y", o, [P, NB, T])
    K.n_so, o = at("n_so", o, [P, 64])


def blocks(t):
    return t.rearrange("p (c l) -> p c l", c=NB)


def pe_gdn(K, pe, pos):
    t = K.nc.tensor
    pe.wait_ge(K.sem("w_lo"), pos.next("w_lo"))
    gemm_tok(K, pos, 0, 256)
    pe.wait_ge(K.sem("w_lo"), pos.next("w_lo"))
    gemm_tok(K, pos, 1, 32, at=256, free=False)
    with pos.loop(2):
        for s in range(2):
            pe.wait_ge(K.sem("w_lo"), pos.next("w_lo"))
            gemm(K, pos, s, (2 * s, 2 * s + 1), K.h_hi, K.h_lo)
            for n in range(2):
                pe.wait_ge(K.sem("head_sq"), pos.next("head_sq"))
                t.matmul(K.p[n][:], K.mask("ones"), K.m_sq[:, n], start=True, stop=True
                    ).then_inc(K.sem("head_sum"), 1)
    for _ in range(2):
        for s in range(2):
            pe.wait_ge(K.sem("w_lo"), pos.next("w_lo"))
            gemm(K, pos, s, (2 * s, 2 * s + 1), K.h_hi, K.h_lo)
    pe.wait_ge(K.sem("m_gl"), pos.next("m_gl"))
    g = K.m_gl[:].rearrange("p c h -> p (c h)")
    t.matmul(K.p[0][:, 0:16], K.mask("tri64"), g, start=True, stop=True)
    t.matmul(K.p[1][:, 0:16], K.mask("bd64"), g, start=True, stop=True).then_inc(K.sem("m_gs"), 1)
    pe.wait_ge(K.sem("m_tok"), pos.next("m_tok"))
    pe.wait_ge(K.sem("m_silu"), pos.next("m_silu", 4))
    for h in range(4):
        for c in range(NB):
            last = t.transpose(K.p[0][:, c * P:c * P + P], K.m_qk[:, 4 + h, c * P:c * P + P], K.mask("ident"))
        last.then_inc(K.sem("m_kt"), 1)
        for c in range(NB):
            last = t.transpose(K.p[1][:, c * P:c * P + P], K.m_vf[:, h, c * P:c * P + P], K.mask("ident"))
        last.then_inc(K.sem("m_vt"), 1)
        for c in range(NB):
            last = t.matmul(K.p[2][:, c * P:c * P + P], K.m_gl[:, c, h:h + 1].broadcast_to([P, P]), K.mask("tri64"),
                            start=True, stop=True)
        last.then_inc(K.sem("m_bc"), 1)
        for c in range(NB):
            last = t.matmul(K.p[3][:, c * P:c * P + P], K.m_sig[:, c, h:h + 1].broadcast_to([P, P]), K.mask("ident"),
                            start=True, stop=True)
        last.then_inc(K.sem("m_bb"), 1)
        pe.wait_ge(K.sem("m_kb"), pos.next("m_kb"))
        for c in range(NB):
            last = t.matmul(K.p[0][:, c * P:c * P + P], K.m_qk[:, 4 + h, c * P:c * P + P], K.t_kb[:, c * P:c * P + P],
                            start=True, stop=True)
        last.then_inc(K.sem("m_kk"), 1)
        for c in range(NB):
            last = t.matmul(K.p[1][:, c * P:c * P + P], K.m_qk[:, 4 + h, c * P:c * P + P],
                            K.m_qk[:, h, c * P:c * P + P], start=True, stop=True)
        last.then_inc(K.sem("m_qkt"), 1)
        pe.wait_ge(K.sem("m_u1"), pos.next("m_u1"))
        for c in range(NB):
            last = t.transpose(K.p[0][:, c * P:c * P + P], K.m_U[:, h, c * P:c * P + P], K.mask("ident"))
        last.then_inc(K.sem("m_t1"), 1)
        for b in (2, 4, 8, 16, 32):
            pe.wait_ge(K.sem("m_m"), pos.next("m_m"))
            for c in range(NB):
                q = slice(c * P, c * P + P)
                last = t.matmul(K.p[0][:, q], K.t_m[:, q], K.t_T[:, q], start=True, stop=True)
            last.then_inc(K.sem("m_mt"), 1)
            pe.wait_ge(K.sem("m_y"), pos.next("m_y"))
            for c in range(NB):
                q = slice(c * P, c * P + P)
                last = t.matmul(K.p[2][:, q], K.t_y[:, q], K.m_U[:, h, q], start=True, stop=True)
            last.then_inc(K.sem("m_yu"), 1)
            if b < 32:
                for c in range(NB):
                    q = slice(c * P, c * P + P)
                    last = t.matmul(K.p[1][:, q], K.m_U[:, h, q], K.t_y[:, q], start=True, stop=True)
                last.then_inc(K.sem("m_ty"), 1)
        pe.wait_ge(K.sem("m_u"), pos.next("m_u"))
        for c in range(NB):
            q = slice(c * P, c * P + P)
            last = t.matmul(K.p[3][:, q], K.m_kbe[:, h, q], K.m_U[:, h, q], start=True, stop=True)
        last.then_inc(K.sem("m_w"), 1)
        pe.wait_ge(K.sem("m_nw"), pos.next("m_nw"))
    pe.sem_inc(pos.own, pos.tick())
    for ch in range(8):
        c, e = ch // 2, ch % 2
        r = slice(64 * e, 64 * e + 64)
        q = slice(c * P, c * P + P)
        qe = slice(c * P + 64 * e, c * P + 64 * e + 64)
        for h in range(4):
            if ch:
                pe.wait_ge(K.sem("m_st"), pos.next("m_st"))
                pe.sem_inc(pos.own, pos.tick())
            last = t.matmul(K.p[h][r, 0:P], K.m_U[r, h, qe], K.m_vb[r, h, q], start=True, stop=ch == 0)
            if ch:
                last = t.matmul(K.p[h][r, 0:P], K.m_nw[:, h, qe], K.m_S[:, h], start=False, stop=True)
            last.then_inc(K.sem("m_vp"), 1)
        for h in range(4):
            pe.wait_ge(K.sem("m_vn"), pos.next("m_vn"))
            t.matmul(K.p[h][:, P:P + 64], K.t_vn[r, h], K.m_at[r, h, qe], start=True, stop=ch == 0)
            if ch:
                t.matmul(K.p[h][:, P:P + 64], K.m_S[:, h], K.m_qk[:, h, qe], start=False, stop=True)
            t.matmul(K.p[h][:, 256:256 + P], K.m_kd[r, h, q], K.t_vn[r, h], start=True, stop=True
                ).then_inc(K.sem("m_sp"), 1)
    pe.wait_ge(K.sem("m_st"), pos.next("m_st", 4))
    for h in range(4):
        pe.wait_ge(K.sem("head_sq"), pos.next("head_sq"))
        t.matmul(K.p[h % 2][:], K.mask("ones"), K.m_sq[:, h % 2], start=True, stop=True
            ).then_inc(K.sem("head_sum"), 1)
    pe.wait_ge(K.sem("m_done"), pos.next("m_done"))


def act_gdn(K, act, pos):
    act.wait_ge(K.sem("part"), pos.next("part", 4))
    split_unit(K, act, pos, 0)
    act.wait_ge(K.sem("part"), pos.next("part", 4))
    split_unit(K, act, pos, 1)
    act.wait_ge(K.sem("m_bag"), pos.next("m_bag"))
    act.activation(K.m_sig[:], K.m_bag[:], ACT.Sigmoid).then_inc(K.sem("m_sig"), 1)
    act.activation(K.m_ea[:], K.rows2[:, 0:4], ACT.Exp).then_inc(K.sem("dt_ea"), 1)
    act.wait_ge(K.sem("dt_n"), pos.next("dt_n"))
    act.activation(K.m_sp[:, 2], K.m_sp[:, 1], ACT.Exp).then_inc(K.sem("dt_e"), 1)
    act.wait_ge(K.sem("dt_u"), pos.next("dt_u"))
    act.activation(K.m_sp[:, 5], K.m_sp[:, 3], ACT.Ln).then_inc(K.sem("dt_l"), 1)
    with pos.loop(2) as w:
        for s in range(2):
            act.wait_ge(K.sem("part"), pos.next("part", 2))
            split_unit(K, act, pos, s)
            for n in range(2):
                x = idx(K.m_qk, w * 4 + 2 * s + n)
                act.wait_ge(K.sem("m_conv"), pos.next("m_conv"))
                act.sem_inc(pos.own, pos.tick())
                act.activation(x, x, ACT.Silu).then_inc(pos.own, pos.tick())
                act.wait_ge(pos.own, pos.ticks())
                act.sem_inc(pos.own, pos.tick())
                act.activation(K.m_sq[:, n], x, ACT.Square).then_inc(K.sem("head_sq"), 1)
            for n in range(2):
                act.wait_ge(K.sem("head_sum"), pos.next("head_sum"))
                act.activation(K.m_rs[:, n], K.p[n][:], ACT.Sqrt, bias=K.col("eps")).then_inc(K.sem("head_std"), 1)
    for s in range(2):
        act.wait_ge(K.sem("part"), pos.next("part", 2))
        split_unit(K, act, pos, s)
        for n in range(2):
            x = K.m_vf[:, 2 * s + n]
            act.wait_ge(K.sem("m_conv"), pos.next("m_conv"))
            act.activation(x, x, ACT.Silu).then_inc(K.sem("m_silu"), 1)
    for s in range(2):
        for n in range(2):
            b = 2 * s + n
            act.wait_ge(K.sem("part"), pos.next("part"))
            act.activation(K.m_z[:, b], K.g[b][:], ACT.Silu).then_inc(pos.own, pos.tick())
            act.wait_ge(pos.own, pos.ticks())
            act.sem_inc(K.sem(f"g_free{b}"), 1)
        split_unit(K, act, pos, s)
    act.wait_ge(K.sem("m_gc"), pos.next("m_gc"))
    act.activation(K.m_dl[:], K.m_dl[:], ACT.Exp).then_inc(pos.own, pos.tick())
    act.wait_ge(pos.own, pos.ticks())
    act.activation(K.m_be[:], K.m_gc[:], ACT.Exp).then_inc(pos.own, pos.tick())
    act.wait_ge(pos.own, pos.ticks())
    act.sem_inc(K.sem("m_ex"), 1)
    for h in range(4):
        act.wait_ge(K.sem("m_bc"), pos.next("m_bc"))
        act.activation(K.t_eb[:], K.p[2][:], ACT.Exp).then_inc(K.sem("m_eb"), 1)
        act.wait_ge(K.sem("m_seg"), pos.next("m_seg"))
        act.activation(K.t_d[:], K.t_d[:], ACT.Exp).then_inc(K.sem("m_dec"), 1)
        act.wait_ge(K.sem("m_t1"), pos.next("m_t1"))
        act.activation(K.t_T[:], K.p[0][:], ACT.Copy).then_inc(K.sem("m_t1c"), 1)
        for b in (2, 4, 8, 16, 32):
            act.wait_ge(K.sem("m_mt"), pos.next("m_mt"))
            act.activation(K.t_y[:], K.p[0][:], ACT.Copy).then_inc(K.sem("m_y"), 1)
        act.wait_ge(K.sem("m_w"), pos.next("m_w"))
        act.activation(K.m_nw[:, h], K.p[3][:], ACT.Copy, scale=-1.0).then_inc(K.sem("m_nw"), 1)
    for ch in range(8):
        r = slice(64 * (ch % 2), 64 * (ch % 2) + 64)
        for h in range(4):
            act.wait_ge(K.sem("m_vp"), pos.next("m_vp"))
            act.activation(K.t_vn[r, h], K.p[h][r, 0:P], ACT.Copy).then_inc(K.sem("m_vn"), 1)
    for h in range(4):
        act.wait_ge(K.sem("m_o"), pos.next("m_o"))
        act.activation(K.m_sq[:, h % 2], K.m_o[:, h], ACT.Square).then_inc(K.sem("head_sq"), 1)
        act.wait_ge(K.sem("head_sum"), pos.next("head_sum"))
        act.activation(K.m_rs[:, h % 2], K.p[h % 2][:], ACT.Sqrt, scale=1.0 / P, bias=K.col("eps")
            ).then_inc(K.sem("head_std"), 1)
        act.wait_ge(K.sem("m_yn"), pos.next("m_yn"))
        act.activation(K.m_yhi[:, h], K.m_o[:, h], ACT.Copy).then_inc(K.sem("m_yh"), 1)


def dve_gdn(K, dve, pos):
    v = K.nc.vector
    pos.skip("part", 4)
    for c in range(NB):
        dve.wait_ge(K.sem("part"), pos.next("part"))
        v.tensor_copy(K.m_v[:, c], K.g[c][:, 0:256]).then_inc(pos.own, pos.tick())
        v.tensor_copy(K.m_bag[:, c], K.g[c][:, 256:288]).then_inc(pos.own, pos.tick())
        dve.wait_ge(pos.own, pos.ticks())
        dve.sem_inc(K.sem(f"g_free{c}"), 1)
    dve.sem_inc(K.sem("m_bag"), 1)
    S = [K.m_sp[:, i] for i in range(7)]
    v.tensor_tensor(S[0].rearrange("p (c h) -> p c h", c=NB), K.m_bag[:, :, 4:8],
                    K.rows2[:, 4:8].unsqueeze(1).broadcast_to([P, NB, 4]), ALU.add).then_inc(pos.own, pos.tick())
    dve.wait_ge(pos.own, pos.ticks())
    softplus(K, pos, S, S[6])
    dve.wait_ge(K.sem("dt_ea"), pos.next("dt_ea"))
    v.scalar_tensor_tensor(K.m_gl[:], S[6].rearrange("p (c h) -> p c h", c=NB), -1.0,
                           K.m_ea[:].unsqueeze(1).broadcast_to([P, NB, 4]), ALU.mult, ALU.mult
        ).then_inc(pos.own, pos.tick())
    dve.wait_ge(pos.own, pos.ticks())
    dve.sem_inc(K.sem("m_gl"), 1)
    with pos.loop(2) as w:
        for s in range(2):
            for n in range(2):
                b = 2 * s + n
                dve.wait_ge(K.sem("part"), pos.next("part"))
                conv(K, pos, idx(K.m_qk, w * 4 + b), K.g[b][:], lambda i: K.col2("conv_w", w * 16 + b * 4 + i),
                     K.col("zero"), 4)
                dve.sem_inc(K.sem("m_conv"), 1)
                dve.sem_inc(K.sem(f"g_free{b}"), 1)
            for n in range(2):
                x = idx(K.m_qk, w * 4 + 2 * s + n)
                dve.wait_ge(K.sem("head_std"), pos.next("head_std"))
                v.reciprocal(K.m_rs[:, n], K.m_rs[:, n]).then_inc(pos.own, pos.tick())
                dve.wait_ge(pos.own, pos.ticks())
                v.scalar_tensor_tensor(x, x, K.col("qks", w), K.m_rs[:, n], ALU.mult, ALU.mult
                    ).then_inc(pos.own, pos.tick())
                dve.wait_ge(pos.own, pos.ticks())
    for b in range(4):
        dve.wait_ge(K.sem("part"), pos.next("part"))
        conv(K, pos, K.m_vf[:, b], K.g[b][:], lambda i: K.col2("conv_w", 32 + b * 4 + i), K.col("zero"), 4)
        dve.sem_inc(K.sem("m_conv"), 1)
        dve.sem_inc(K.sem(f"g_free{b}"), 1)
    pos.skip("part", 4)
    dve.wait_ge(K.sem("m_gs"), pos.next("m_gs"))
    v.tensor_copy(K.m_gc[:].rearrange("p c h -> p (c h)"), K.p[0][:, 0:16]).then_inc(pos.own, pos.tick())
    dve.wait_ge(pos.own, pos.ticks())
    v.tensor_tensor(K.m_dl[:].rearrange("p c h -> p (c h)"), K.p[1][:, 0:16],
                    K.m_gc[:].rearrange("p c h -> p (c h)"), ALU.subtract).then_inc(pos.own, pos.tick())
    dve.wait_ge(pos.own, pos.ticks())
    dve.sem_inc(K.sem("m_gc"), 1)
    dve.wait_ge(K.sem("m_ex"), pos.next("m_ex"))
    dve.wait_ge(K.sem("m_sig"), pos.next("m_sig"))
    v.tensor_tensor(K.m_be[:], K.m_be[:], K.m_sig[:, :, 0:4], ALU.mult).then_inc(pos.own, pos.tick())
    dve.wait_ge(pos.own, pos.ticks())
    dve.sem_inc(K.sem("m_tok"), 1)

    def per_token(t, h):
        return t[:, :, h:h + 1].broadcast_to([P, NB, P])
    for h in range(4):
        dve.wait_ge(K.sem("m_kt"), pos.next("m_kt"))
        v.tensor_tensor(blocks(K.m_kbe[:, h]), blocks(K.p[0][:]), per_token(K.m_be, h), ALU.mult
            ).then_inc(pos.own, pos.tick())
        v.tensor_tensor(blocks(K.m_kd[:, h]), blocks(K.p[0][:]), per_token(K.m_dl, h), ALU.mult
            ).then_inc(pos.own, pos.tick())
        dve.wait_ge(K.sem("m_vt"), pos.next("m_vt"))
        v.tensor_tensor(blocks(K.m_vb[:, h]), blocks(K.p[1][:]), per_token(K.m_sig, h), ALU.mult
            ).then_inc(pos.own, pos.tick())
        dve.wait_ge(K.sem("m_bb"), pos.next("m_bb"))
        v.tensor_tensor(K.t_kb[:], K.m_qk[:, 4 + h], K.p[3][:], ALU.mult).then_inc(pos.own, pos.tick())
        dve.wait_ge(pos.own, pos.ticks())
        dve.sem_inc(K.sem("m_kb"), 1)
        dve.wait_ge(K.sem("m_eb"), pos.next("m_eb"))
        v.tensor_copy(K.m_el[:, h], K.t_eb[:, 63::64]).then_inc(pos.own, pos.tick())
        for c in range(NB):
            v.tensor_scalar(K.t_d[:, c * P:c * P + P], K.p[2][:, c * P:c * P + P], K.m_gc[:, c, h:h + 1], 0.0,
                            ALU.subtract, ALU.min).then_inc(pos.own, pos.tick())
        dve.wait_ge(pos.own, pos.ticks())
        dve.sem_inc(K.sem("m_seg"), 1)
        dve.wait_ge(K.sem("m_dec"), pos.next("m_dec"))
        dve.wait_ge(K.sem("m_kk"), pos.next("m_kk"))
        v.tensor_tensor(K.t_l[:], K.p[0][:], K.t_d[:], ALU.mult).then_inc(pos.own, pos.tick())
        dve.wait_ge(pos.own, pos.ticks())
        mask = lambda name: K.mask(name).unsqueeze(1).broadcast_to([P, NB, P])
        U = K.m_U[:, h]
        v.tensor_tensor(blocks(U), blocks(K.t_l[:]), mask("inv1"), ALU.mult).then_inc(pos.own, pos.tick())
        dve.wait_ge(pos.own, pos.ticks())
        v.scalar_tensor_tensor(blocks(U), blocks(U), -1.0, mask("ident"), ALU.mult, ALU.add
            ).then_inc(pos.own, pos.tick())
        dve.wait_ge(pos.own, pos.ticks())
        dve.sem_inc(K.sem("m_u1"), 1)
        dve.wait_ge(K.sem("m_qkt"), pos.next("m_qkt"))
        v.tensor_tensor(K.m_at[:, h], K.p[1][:], K.t_d[:], ALU.mult).then_inc(pos.own, pos.tick())
        dve.wait_ge(pos.own, pos.ticks())
        v.tensor_tensor(blocks(K.m_at[:, h]), blocks(K.m_at[:, h]), mask("tri64"), ALU.mult
            ).then_inc(pos.own, pos.tick())
        dve.wait_ge(pos.own, pos.ticks())
        v.tensor_tensor(K.m_qk[:, h], K.m_qk[:, h], K.t_eb[:], ALU.mult).then_inc(pos.own, pos.tick())
        dve.wait_ge(pos.own, pos.ticks())
        dve.wait_ge(K.sem("m_t1c"), pos.next("m_t1c"))
        for b in (2, 4, 8, 16, 32):
            v.tensor_tensor(blocks(K.t_m[:]), blocks(K.t_l[:]), mask(f"inv{b}"), ALU.mult
                ).then_inc(pos.own, pos.tick())
            dve.wait_ge(pos.own, pos.ticks())
            dve.sem_inc(K.sem("m_m"), 1)
            dve.wait_ge(K.sem("m_yu"), pos.next("m_yu"))
            if b < 32:
                dve.wait_ge(K.sem("m_ty"), pos.next("m_ty"))
                v.tensor_tensor(K.t_T[:], K.t_T[:], K.p[1][:], ALU.subtract).then_inc(pos.own, pos.tick())
                dve.wait_ge(pos.own, pos.ticks())
            v.tensor_tensor(U, U, K.p[2][:], ALU.subtract).then_inc(pos.own, pos.tick())
            dve.wait_ge(pos.own, pos.ticks())
        dve.sem_inc(K.sem("m_u"), 1)
    for ch in range(8):
        c, e = ch // 2, ch % 2
        for h in range(4):
            dve.wait_ge(K.sem("m_sp"), pos.next("m_sp"))
            if ch:
                v.scalar_tensor_tensor(K.m_S[:, h], K.m_S[:, h], K.m_el[:, h, ch:ch + 1], K.p[h][:, 256:256 + P],
                                       ALU.mult, ALU.add).then_inc(pos.own, pos.tick())
            else:
                v.tensor_copy(K.m_S[:, h], K.p[h][:, 256:256 + P]).then_inc(pos.own, pos.tick())
            v.tensor_copy(K.m_o[:, h, c * P + 64 * e:c * P + 64 * e + 64], K.p[h][:, P:P + 64]
                ).then_inc(pos.own, pos.tick())
            dve.wait_ge(pos.own, pos.ticks())
            dve.sem_inc(K.sem("m_st"), 1)
    for h in range(4):
        dve.sem_inc(K.sem("m_o"), 1)
    for h in range(4):
        x = K.m_o[:, h]
        dve.wait_ge(K.sem("head_std"), pos.next("head_std"))
        v.reciprocal(K.m_rs[:, h % 2], K.m_rs[:, h % 2]).then_inc(pos.own, pos.tick())
        dve.wait_ge(pos.own, pos.ticks())
        v.scalar_tensor_tensor(x, x, K.col2("gdn_norm"), K.m_rs[:, h % 2], ALU.mult, ALU.mult
            ).then_inc(pos.own, pos.tick())
        dve.wait_ge(pos.own, pos.ticks())
        v.tensor_tensor(x, x, K.m_z[:, h], ALU.mult).then_inc(pos.own, pos.tick())
        dve.wait_ge(pos.own, pos.ticks())
        dve.sem_inc(K.sem("m_yn"), 1)
        dve.wait_ge(K.sem("m_yh"), pos.next("m_yh"))
        v.tensor_tensor(K.m_ylo[:, h], x, K.m_yhi[:, h].bitcast(F32), ALU.subtract).then_inc(pos.own, pos.tick())
        dve.wait_ge(pos.own, pos.ticks())
    dve.sem_inc(K.sem("m_done"), 1)
    dve.sem_inc(K.sem("m_free"), 1)



def pe_nsa(K, pe, pos):
    t = K.nc.tensor
    pe.wait_ge(K.sem("n_trig"), pos.next("n_trig"))
    for tile in range(8):
        if tile % 2 == 0:
            pe.wait_ge(K.sem("w_lo"), pos.next("w_lo"))
            b = tile % 4
            gemm(K, pos, (tile // 2) % 2, (b, b + 1), K.h_hi, K.h_lo)
        if tile != 5:
            pe.wait_ge(K.sem("n_raw"), pos.next("n_raw"))
            t.matmul(K.p[0][:], K.mask("swap"), K.n_raw[:], start=True, stop=True).then_inc(K.sem("n_swap"), 1)
            pe.wait_ge(K.sem("n_rot"), pos.next("n_rot"))
    pe.wait_ge(K.sem("n_w1"), pos.next("n_w1", 64))
    for kv in range(2):
        pe.wait_ge(K.sem("n_blk"), pos.next("n_blk"))
        for G in range(2):
            r = slice(64 * G, 64 * G + 64)
            for l in range(32):
                last = t.matmul(K.p[G][:, 0:31], K.n_w1[r, kv, l], K.n_blk[r, l, 0:31], start=l == 0, stop=l == 31)
            last.then_inc(K.sem("n_h"), 1)
        for G in range(2):
            pe.wait_ge(K.sem("n_hid"), pos.next("n_hid"))
        for G in range(2):
            if kv == 0:
                last = t.matmul(K.p[2][64 * G:64 * G + 64, 0:31], K.col2("w2k", 0, 64), K.n_hid[:, G, 0:31],
                                start=True, stop=True)
            else:
                last = t.matmul(K.p[2][0:31, 64 * G:64 * G + 64], K.n_hid[:, G, 0:31], K.col2("w2v", 0, 64),
                                start=True, stop=True)
        last.then_inc(K.sem("n_cp"), 1)
        pe.wait_ge(K.sem("n_cc"), pos.next("n_cc"))
    with pos.loop(4):
        pe.wait_ge(K.sem("n_qs"), pos.next("n_qs"))
        for G in range(2):
            r = slice(64 * G, 64 * G + 64)
            for qb in range(NB):
                q, w = K.n_qs[r, qb * P:qb * P + P], (qb + 1) * P
                t.matmul(K.p[0][:, 0:31], q, K.n_kc[r, 0:31], start=True, stop=True)
                t.matmul(K.p[1][:, 0:w], q, K.n_k[r, 2, 0:w], start=True, stop=True)
                t.matmul(K.p[2][:, 0:w], q, K.n_k[r, 3, 0:w], start=True, stop=True).then_inc(K.sem("scores"), 1)
                pe.wait_ge(K.sem("n_ps"), pos.next("n_ps"))
                n = 1 + 2 * (qb + 1)
                for i in range(n):
                    out = K.p[(3, 0, 1)[i // 4]][:, (i % 4) * P:(i % 4) * P + P]
                    if i == 0:
                        last = t.transpose(out[0:31, :], K.n_p[:, 0:31], K.mask("ident"))
                    else:
                        last = t.transpose(out, K.n_p[:, 32 + (i - 1) * P:32 + i * P], K.mask("ident"))
                    if i % 4 == 3 or i == n - 1:
                        last.then_inc(K.sem("probs_t"), 1)
                for i in range(n):
                    if i % 4 == 0:
                        pe.wait_ge(K.sem("probs_t_read"), pos.next("probs_t_read"))
                    if i == 0:
                        last = t.matmul(K.p[2][:, 0:64], K.n_pt[0:31, 0], K.n_vc[0:31, G], start=True, stop=False)
                    else:
                        kb, win = (i - 1) % (qb + 1), (i - 1) // (qb + 1)
                        last = t.matmul(K.p[2][:, 0:64], K.n_pt[:, i], K.m_v[:, kb, P * win + 64 * G:P * win + 64 * G + 64],
                                        start=False, stop=i == n - 1)
                last.then_inc(K.sem("n_o"), 1)
                pe.wait_ge(K.sem("n_out"), pos.next("n_out"))
    for f in range(4):
        for qb in range(NB):
            last = t.transpose(K.p[f][:, qb * P:qb * P + P], K.n_y[:, qb, f * P:f * P + P], K.mask("ident"))
        last.then_inc(K.sem("yt"), 1)
    pe.wait_ge(K.sem("yt_lo"), pos.next("yt_lo", 4))
    with pos.loop(2):
        for s in range(2):
            pe.wait_ge(K.sem("w_lo"), pos.next("w_lo"))
            gemm(K, pos, s, (2 * s, 2 * s + 1), K.m_yhi, K.m_ylo)


def act_nsa(K, act, pos):
    act.wait_ge(K.sem("m_free"), pos.next("m_free"))
    act.dma_start(K.n_pos[:], K.a["pos"].broadcast_to([P, T])).then_inc(K.sem("n_pos"), 16)
    for kv in range(2):
        for G in range(2):
            act.dma_start(K.n_w1[64 * G:64 * G + 64, kv], K.a["w1"][bass.ds(pos.layer * 2 + kv, 1)]
                          .rearrange("a p l c -> p (a l) c")).then_inc(K.sem("n_w1"), 16)
    act.wait_ge(K.sem("n_red"), pos.next("n_red"))
    act.activation(K.n_sin[:], K.n_sin[:], ACT.Sin).then_inc(K.sem("n_tr"), 1)
    act.activation(K.n_cos[:], K.n_cos[:], ACT.Sin).then_inc(K.sem("n_tr"), 1)
    for tile in range(8):
        act.wait_ge(K.sem("part"), pos.next("part"))
        if tile != 5:
            act.activation(K.n_raw[:], K.g[tile % 4][:], ACT.Copy).then_inc(pos.own, pos.tick())
            act.wait_ge(pos.own, pos.ticks())
            act.sem_inc(K.sem("n_raw"), 1)
            act.sem_inc(K.sem(f"g_free{tile % 4}"), 1)
        else:
            act.activation(K.n_k[:, 1], K.g[1][:], ACT.Copy).then_inc(pos.own, pos.tick())
            act.wait_ge(pos.own, pos.ticks())
            act.sem_inc(K.sem("n_vcin"), 1)
            act.sem_inc(K.sem("g_free1"), 1)
        if tile % 2:
            split_unit(K, act, pos, (tile // 2) % 2)
        if tile != 5:
            act.wait_ge(K.sem("n_rota"), pos.next("n_rota"))
    for kv in range(2):
        for G in range(2):
            act.wait_ge(K.sem("n_h"), pos.next("n_h"))
            act.activation(K.n_hid[:, G, 0:31], K.p[G][:, 0:31], ACT.Silu).then_inc(K.sem("n_hid"), 1)
        act.wait_ge(K.sem("n_cp"), pos.next("n_cp"))
        if kv == 0:
            act.activation(K.n_kc[:, 0:31], K.p[2][:, 0:31], ACT.Copy).then_inc(pos.own, pos.tick())
            act.wait_ge(pos.own, pos.ticks())
        else:
            act.activation(K.n_vc[0:31].rearrange("p g d -> p (g d)"), K.p[2][0:31, 0:P], ACT.Copy
                ).then_inc(pos.own, pos.tick())
            act.wait_ge(pos.own, pos.ticks())
        act.sem_inc(K.sem("n_cc"), 1)
    with pos.loop(4) as j:
        act.activation(K.n_qs[:], idx(K.n_q, j), ACT.Copy).then_inc(K.sem("n_qs"), 1)
        for G in range(2):
            for qb in range(NB):
                w = (qb + 1) * P
                s = K.n_stat
                act.wait_ge(K.sem("row_max"), pos.next("row_max"))
                act.activation(K.n_p[:, 0:31], K.p[0][:, 0:31], ACT.Exp, scale=0.125, bias=s[:, 4:5], accum_out=s[:, 8:9])
                act.activation(K.n_p[:, 32:32 + w], K.p[1][:, 0:w], ACT.Exp, scale=0.125, bias=s[:, 5:6],
                               accum_out=s[:, 9:10])
                act.activation(K.n_p[:, 32 + w:32 + 2 * w], K.p[2][:, 0:w], ACT.Exp, scale=0.125, bias=s[:, 6:7],
                               accum_out=s[:, 10:11]).then_inc(K.sem("n_pe"), 1)
                n = 1 + 2 * (qb + 1)
                for i in range(0, n, 4):
                    k = min(4, n - i)
                    act.wait_ge(K.sem("probs_t"), pos.next("probs_t"))
                    src = K.p[(3, 0, 1)[i // 4]]
                    if i == 0:
                        act.activation(K.n_pt[0:31, 0], src[0:31, 0:P], ACT.Copy)
                        act.activation(K.n_pt[:, 1:k].rearrange("p a b -> p (a b)"), src[:, P:k * P], ACT.Copy
                            ).then_inc(K.sem("probs_t_read"), 1)
                    else:
                        act.activation(K.n_pt[:, i:i + k].rearrange("p a b -> p (a b)"), src[:, 0:k * P], ACT.Copy
                            ).then_inc(K.sem("probs_t_read"), 1)
                act.wait_ge(K.sem("n_o"), pos.next("n_o"))
                act.activation(K.n_so[:], K.p[2][:, 0:64], ACT.Square, accum_out=s[:, 12:13]
                    ).then_inc(pos.own, pos.tick())
                act.wait_ge(pos.own, pos.ticks())
                act.activation(s[:, 13:14], s[:, 12:13], ACT.Sqrt, scale=1.0 / 64, bias=K.col("eps")
                    ).then_inc(K.sem("n_std"), 1)
    for f in range(4):
        act.wait_ge(K.sem("yt"), pos.next("yt"))
        act.activation(K.m_yhi[:, 4 + f], K.p[f][:], ACT.Copy).then_inc(K.sem("yt_hi"), 1)
    act_out(K, act, pos)


TWO_PI = (6.28125, 0.0019350051879882812, 3.01991598e-07)
PI = 3.14159250


def dve_nsa(K, dve, pos):
    v = K.nc.vector
    dve.wait_ge(K.sem("n_pos"), pos.next("n_pos", 16))
    v.tensor_copy(K.n_sin[:], K.n_pos[:]).then_inc(pos.own, pos.tick())
    dve.wait_ge(pos.own, pos.ticks())
    v.tensor_scalar(K.n_sin[:], K.n_sin[:], K.col("freq"), None, ALU.mult).then_inc(pos.own, pos.tick())
    dve.wait_ge(pos.own, pos.ticks())
    v.tensor_scalar(K.n_pos[:], K.n_sin[:], 1.0 / (2 * np.pi), None, ALU.mult).then_inc(pos.own, pos.tick())
    dve.wait_ge(pos.own, pos.ticks())
    v.tensor_copy(K.n_cos[:], K.n_pos[:]).then_inc(pos.own, pos.tick())
    dve.wait_ge(pos.own, pos.ticks())
    for c in TWO_PI:
        v.scalar_tensor_tensor(K.n_sin[:], K.n_cos[:], -c, K.n_sin[:], ALU.mult, ALU.add
            ).then_inc(pos.own, pos.tick())
        dve.wait_ge(pos.own, pos.ticks())
    v.tensor_scalar(K.n_sin[:], K.n_sin[:], PI, -PI, ALU.min, ALU.max).then_inc(pos.own, pos.tick())
    dve.wait_ge(pos.own, pos.ticks())
    v.scalar_tensor_tensor(K.n_cos[:], K.n_sin[:], -1.0, K.n_sin[:], ALU.mult, ALU.min).then_inc(pos.own, pos.tick())
    dve.wait_ge(pos.own, pos.ticks())
    v.tensor_scalar(K.n_cos[:], K.n_cos[:], np.pi / 2, None, ALU.add).then_inc(pos.own, pos.tick())
    dve.wait_ge(pos.own, pos.ticks())
    dve.sem_inc(K.sem("n_red"), 1)
    dve.wait_ge(K.sem("n_tr"), pos.next("n_tr", 2))
    v.tensor_scalar(K.n_sin[:], K.n_sin[:], K.col("rots"), None, ALU.mult).then_inc(pos.own, pos.tick())
    dve.wait_ge(pos.own, pos.ticks())
    dve.sem_inc(K.sem("n_trig"), 1)
    for tile in range(8):
        pos.skip("part")
        if tile == 5:
            continue
        dst = K.n_q[:, tile] if tile < 4 else K.n_k[:, tile - 4]
        dve.wait_ge(K.sem("n_swap"), pos.next("n_swap"))
        v.tensor_tensor(dst, K.n_raw[:], K.n_cos[:], ALU.mult).then_inc(pos.own, pos.tick())
        dve.wait_ge(pos.own, pos.ticks())
        v.tensor_tensor(K.n_tmp[:], K.p[0][:], K.n_sin[:], ALU.mult).then_inc(pos.own, pos.tick())
        dve.wait_ge(pos.own, pos.ticks())
        dve.sem_inc(K.sem("n_rot"), 1)
        dve.sem_inc(K.sem("n_rota"), 1)
        v.tensor_tensor(dst, dst, K.n_tmp[:], ALU.add).then_inc(pos.own, pos.tick())
        dve.wait_ge(pos.own, pos.ticks())
    for kv in range(2):
        if kv:
            dve.wait_ge(K.sem("n_vcin"), pos.next("n_vcin"))
            dve.wait_ge(K.sem("n_h"), pos.next("n_h", 2))
        for half in range(2):
            v.tensor_tensor(K.n_blk[:, 16 * half:16 * half + 16, 0:31],
                            K.n_k[:, kv].rearrange("p (n s) -> p s n", s=16)[:, :, half:half + 31],
                            K.col2("pe", 32 * kv + 16 * half, 16).unsqueeze(2).broadcast_to([P, 16, 31]), ALU.add
                ).then_inc(pos.own, pos.tick())
            dve.wait_ge(pos.own, pos.ticks())
        dve.sem_inc(K.sem("n_blk"), 1)
    pos.skip("n_h", 2)
    with pos.loop(4) as j:
        for G in range(2):
            for qb in range(NB):
                w = (qb + 1) * P
                s, m0 = K.n_stat, MI["cmp"]
                dve.wait_ge(K.sem("scores"), pos.next("scores"))
                v.tensor_tensor(K.p[0][:, 0:31], K.p[0][:, 0:31], K.masks[:, m0, qb * 32:qb * 32 + 31], ALU.add
                    ).then_inc(pos.own, pos.tick())
                for i in (1, 2):
                    v.tensor_tensor(K.p[i][:, w - P:w], K.p[i][:, w - P:w], K.mask("causal"), ALU.add
                        ).then_inc(pos.own, pos.tick())
                dve.wait_ge(pos.own, pos.ticks())
                for i in range(3):
                    v.reduce_max(s[:, i:i + 1], K.p[i][:, 0:(31 if i == 0 else w)], AX).then_inc(pos.own, pos.tick())
                dve.wait_ge(pos.own, pos.ticks())
                v.tensor_scalar(s[:, 4:7], s[:, 0:3], NEG / 10, -0.125, ALU.max, ALU.mult
                    ).then_inc(pos.own, pos.tick())
                dve.wait_ge(pos.own, pos.ticks())
                dve.sem_inc(K.sem("row_max"), 1)
                dve.wait_ge(K.sem("n_pe"), pos.next("n_pe"))
                v.tensor_scalar(s[:, 8:11], s[:, 8:11], 1e-30, None, ALU.max).then_inc(pos.own, pos.tick())
                dve.wait_ge(pos.own, pos.ticks())
                v.reciprocal(s[:, 8:11], s[:, 8:11]).then_inc(pos.own, pos.tick())
                dve.wait_ge(pos.own, pos.ticks())
                v.tensor_tensor(s[:, 8:11], s[:, 8:11], K.m_sig[:, qb, bass.ds(j * 3 + 8 + 12 * G, 3)], ALU.mult
                    ).then_inc(pos.own, pos.tick())
                dve.wait_ge(pos.own, pos.ticks())
                for i, c in enumerate((slice(0, 31), slice(32, 32 + w), slice(32 + w, 32 + 2 * w))):
                    v.tensor_scalar(K.n_p[:, c], K.n_p[:, c], s[:, 8 + i:9 + i], None, ALU.mult
                        ).then_inc(pos.own, pos.tick())
                dve.wait_ge(pos.own, pos.ticks())
                dve.sem_inc(K.sem("n_ps"), 1)
                dve.wait_ge(K.sem("n_std"), pos.next("n_std"))
                v.reciprocal(s[:, 14:15], s[:, 13:14]).then_inc(pos.own, pos.tick())
                dve.wait_ge(pos.own, pos.ticks())
                v.scalar_tensor_tensor(K.n_y[:, qb, bass.ds(j * 64 + 256 * G, 64)], K.p[2][:, 0:64], s[:, 14:15],
                                       K.rows2[:, 8:72], ALU.mult, ALU.mult).then_inc(pos.own, pos.tick())
                dve.wait_ge(pos.own, pos.ticks())
                dve.sem_inc(K.sem("n_out"), 1)
    for f in range(4):
        dve.wait_ge(K.sem("yt_hi"), pos.next("yt_hi"))
        v.tensor_tensor(K.m_ylo[:, 4 + f], K.p[f][:], K.m_yhi[:, 4 + f].bitcast(F32), ALU.subtract
            ).then_inc(pos.own, pos.tick())
        dve.wait_ge(pos.own, pos.ticks())
        dve.sem_inc(K.sem("yt_lo"), 1)
    dve_out(K, dve, pos, gate_of(K, 1))

PARTS = dict(
    start=(pe_start, act_start, dve_start),
    norm1=norm_parts("norm1"), dt=(pe_dt, act_dt, dve_dt), ssd=(pe_ssd, act_ssd, dve_ssd), z=(pe_z, act_z, dve_z),
    gssd=(pe_gssd, act_gssd, dve_gssd), att=(pe_att, act_att, dve_att), aproj=(pe_aproj, act_aproj, dve_aproj),
    out=(pe_out, act_out, dve_out), norm2=norm_parts("norm2"),
    ffn=(pe_ffn, lambda K, e, p: act_ffn(K, e, p, True), lambda K, e, p: dve_ffn(K, e, p, True, None)),
    ada=(pe_ada, act_ada, dve_ada), norm_a=mod_norm_parts(0), norm_b=mod_norm_parts(1), norm_c=mod_norm_parts(2),
    ffn_a=(pe_ffn, lambda K, e, p: act_ffn(K, e, p, False), lambda K, e, p: dve_ffn(K, e, p, False, gate_of(K, 0))),
    ffn_c=(pe_ffn, lambda K, e, p: act_ffn(K, e, p, False), lambda K, e, p: dve_ffn(K, e, p, False, gate_of(K, 2))),
    gdn=(pe_gdn, act_gdn, dve_gdn), nsa=(pe_nsa, act_nsa, dve_nsa), final=(pe_final, act_final, dve_final))
PE_PARTS, ACT_PARTS, DVE_PARTS = ({k: v[i] for k, v in PARTS.items()} for i in range(3))
PAIRS = dict(dt=UR_DT, ssd=UR_SSD, z=UR_Z, gssd=UR_GSSD + UR_SPROJ, att=UR_ATT, aproj=UR_APROJ, out=UR_OUT,
             ffn=UR_UP + UR_DOWN, ffn_a=UR_UP + UR_DOWN, ffn_c=UR_UP + UR_DOWN, gdn=5, nsa=4)


def plan_pairs(plan):
    n = [sum(PAIRS.get(p, 0) for p in q) for q in plan]
    return n[0] + LAYERS * n[1] + n[2] + 1



def unit(w, width):
    k = w.shape[0] // P
    u = w.reshape(k, P, width).transpose(1, 0, 2).reshape(P, k * width)
    out = np.zeros((P, UNIT), np.float32)
    out[:, :k * width] = u
    return out


def padded(w, width=256):
    out = np.zeros((w.shape[0], width), np.float32)
    out[:, :w.shape[1]] = w
    return out


def up_units(w):
    return [unit(np.concatenate([w[:, j * P:j * P + P], w[:, FF + j * P:FF + j * P + P]], 1), 256) for j in range(NJ)]


def down_units(w):
    return [unit(w[11 * P * h:11 * P * (h + 1), m * P:m * P + P], P) for m in range(KD) for h in range(2)]


def plain_units(w, width=256):
    return [unit(w[:, c:c + width], width) for c in range(0, w.shape[1], width)]


def first_stream(w_in, w_ssd_proj, w_attn_proj, w_out, w_up, w_down):
    z, xbc, dt, q, k, v, gs, ga = np.split(w_in, np.cumsum((2048, 4096, 32, 1536, 1536, 1536, 1024)), axis=1)
    u = [unit(padded(dt), 256), np.zeros((P, UNIT), np.float32)]
    for g in range(GROUPS):
        u.append(unit(xbc[:, 256 * g:256 * g + 256], 256))
        u.append(unit(np.concatenate([xbc[:, 2048 + P * g:2048 + P * g + P], xbc[:, 3072 + P * g:3072 + P * g + P]], 1), 256))
    u += plain_units(z) + plain_units(gs) + plain_units(w_ssd_proj, P)
    for j in range(4):
        def cut(w, g):
            return w[:, 512 * g + P * j:512 * g + P * j + P]
        u += [unit(np.concatenate([cut(q, g), cut(k, g)], 1), 256) for g in range(3)]
        u.append(unit(np.concatenate([cut(v, 0), cut(v, 1)], 1), 256))
        u.append(unit(np.concatenate([cut(v, 2), ga[:, 256 * j:256 * j + P]], 1), 256))
        u.append(unit(padded(ga[:, 256 * j + P:256 * j + 256]), 256))
    u += plain_units(w_attn_proj, 512) + plain_units(w_out) + up_units(w_up) + down_units(w_down)
    return u


def col(v):
    return v.reshape(-1, P).T


def masks():
    i, j = np.arange(P)[:, None], np.arange(P)[None, :]
    m = {"ident": i == j, "ones": i >= 0 * j, "tri": i <= j, "bd64": i // 64 == j // 64,
         "tri64": (i <= j) & (i // 64 == j // 64)}
    for b in (1, 2, 4, 8, 16, 32):
        m[f"inv{b}"] = (i < j) & (i // b != j // b) & (i // (2 * b) == j // (2 * b))
    m["swap"] = (i // 16 == j // 16) & (i % 64 < 16) & ((i + 8) % 16 == j % 16)
    out = {k: v.astype(np.float32) for k, v in m.items()}
    for name, ok in (("causal", j <= i), ("band", j >= i)):
        out[name] = np.where(ok, 0.0, NEG).astype(np.float32)
    for d in (4, 16):
        out[f"mod{d}"] = np.where((i - j) % d == 0, 0.0, NEG).astype(np.float32)
        out[f"mod{d}c"] = np.where(((i - j) % d == 0) & (j <= i), 0.0, NEG).astype(np.float32)
    n, qb = j % 32, j // 32
    out["cmp"] = np.where((n < 31) & (16 * n + 31 <= qb * P + i), 0.0, NEG).astype(np.float32)
    return np.stack([out[k] for k in MASKS], 1)


def first_columns(b):
    j = np.arange(P) % 64
    freq = np.where(j < 16, np.float32(500000.0) ** -(np.float32(2.0 / 16) * (j % 8).astype(np.float32)), 0)
    rot = j < 16
    order = [x for g in range(GROUPS) for x in (2 * g, 2 * g + 1, 16 + g, 24 + g)]
    cw = b["ssd_conv_w"][0].reshape(4, 32, P)[:, order].transpose(2, 1, 0).reshape(P, 128)
    cb = b["ssd_conv_b"][0].reshape(32, P)[order].T
    ffo = [x for t in range(NJ) for x in (t, NJ + t)]
    fw = b["ffn_conv_w"][0].reshape(3, 2 * NJ, P)[:, ffo].transpose(2, 1, 0).reshape(P, NJ * 6)
    fb = b["ffn_conv_b"][0].reshape(2 * NJ, P)[ffo].T
    one = np.ones((P, 1), np.float32)
    parts = dict(zero=0 * one, eps=EPS * one, norm1=col(b["norm1_g"][0]), conv_w=cw, conv_b=cb,
                 dskip=col(np.repeat(b["d_skip"][0], 64)), ssd_norm=col(b["ssd_norm_g"][0]),
                 qg=col(np.concatenate([b["q_norm_g"][0]] * 2)), kg=col(np.concatenate([b["k_norm_g"][0]] * 2)),
                 norm2=col(b["norm2_g"][0]), ffn_w=fw, ffn_b=fb, cvec=col(b["c_2"][0]),
                 qks=np.concatenate([one * 128 ** -0.5, one], 1),
                 freq=freq.astype(np.float32)[:, None], rots=np.where(rot, np.where(j < 8, -1.0, 1.0), 0).astype(np.float32)[:, None],
                 final=col(b["final_norm_g_2"]))
    out = np.concatenate([parts[k] for k in C1], 1).astype(np.float32)
    assert out.shape == (P, NC1)
    return out


def layer_stream(ffn_w_in, ffn_w_out, mix_w_in, mix_w_out):
    qkv, z, b, a, q, kc, vc, ks, vs, kw, vw, g = np.split(
        mix_w_in, np.cumsum((1536, 512, 4, 4, 512, 128, 128, 128, 128, 128, 128)), axis=1)
    cat = lambda *w: np.concatenate(w, 1)
    q = cat(*(q[:, h * 64:h * 64 + 64] for j in range(4) for h in (j, j + 4)))
    u = up_units(ffn_w_in[0]) + down_units(ffn_w_out[0])
    u += [unit(cat(vs, vw), 256), unit(padded(cat(b, a, g)), 256)]
    u += plain_units(qkv) + plain_units(z) + plain_units(q) + [unit(cat(kc, vc), 256), unit(cat(ks, kw), 256)]
    u += plain_units(mix_w_out)
    return u + up_units(ffn_w_in[1]) + down_units(ffn_w_out[1])


def layer_columns(b, l):
    twice = lambda w: np.concatenate([w, w], 0)
    parts = dict(norm=np.concatenate([col(b["norm_g_2"][l, i]) for i in range(3)], 1), adab=col(b["ada_b_2"][l]),
                 conv_w=b["gdn_conv_w_2"][l].reshape(4, 12, P).transpose(2, 1, 0).reshape(P, 48),
                 gdn_norm=b["gdn_norm_g_2"][l][:, None],
                 pe=np.concatenate([twice(b["cmp_pe_k_2"][l].T), twice(b["cmp_pe_v_2"][l].T)], 1),
                 w2k=b["cmp_w2_k_2"][l], w2v=b["cmp_w2_v_2"][l])
    out = np.concatenate([parts[k] for k in C2], 1).astype(np.float32)
    assert out.shape == (P, NC2)
    return out


def layout(b):
    units = first_stream(*(b[n][0] for n in ("w_in", "w_ssd_proj", "w_attn_proj", "w_out", "w_up", "w_down")))
    assert len(units) == 2 * UR1, (len(units), UR1)
    ada = []
    for l in range(LAYERS):
        units += layer_stream(b["ffn_w_in_2"][l], b["ffn_w_out_2"][l], b["mix_w_in_2"][l], b["mix_w_out_2"][l])
        ada += plain_units(b["ada_w_2"][l])
    assert len(units) == 2 * NUR, (len(units), NUR)
    units += [np.zeros((P, UNIT), np.float32)] * 2
    w1 = [b[n][l].reshape(32, 64, P).transpose(1, 0, 2) for l in range(LAYERS) for n in ("cmp_w1_k_2", "cmp_w1_v_2")]
    return dict(stream=np.stack(units), ada=np.stack(ada), masks=masks(), cols1=first_columns(b),
                cols2=np.stack([layer_columns(b, l) for l in range(LAYERS)]),
                rows1=np.concatenate([b["dt_bias"][0], b["a_log"][0]])[None],
                rows2=np.stack([np.concatenate([b["gdn_a_log_2"][l], b["gdn_dt_bias_2"][l], b["nsa_norm_g_2"][l]])
                                for l in range(LAYERS)]),
                w1=np.stack(w1), pos=b["positions_2"].astype(np.int32),
                x=np.ascontiguousarray(b["x"][0].T.reshape(KD, P, T).transpose(1, 0, 2)))


PLAN = (["norm1", "dt", "ssd", "z", "gssd", "att", "aproj", "out", "norm2", "ffn"],
        ["ada", "norm_a", "ffn_a", "norm_b", "gdn", "nsa", "norm_c", "ffn_c"], ["final"])


def kernel(**inputs):
    import concourse.bacc as _bacc
    from concourse.bass_utils import run_bass_kernel_spmd as _run

    b = {k: np.asarray(v) for k, v in inputs.items()}
    arrays = layout(b)
    maker = lambda: _bacc.Bacc("TRN2", target_bir_lowering=False, num_devices=1)

    def made(nc, sizes):
        aps = {name: nc.dram_tensor(f"in_{name}", v.shape, mybir.dt.from_np(v.dtype), kind="ExternalInput").ap()
               for name, v in arrays.items()}
        aps["out"] = nc.dram_tensor("out_x", (P, KD, T), F32, kind="ExternalOutput").ap()
        return build(nc, aps, PLAN, sizes)

    sizes = made(maker(), None)
    nc = maker()
    made(nc, sizes)
    r = _run(nc, [{f"in_{k}": v for k, v in arrays.items()}], core_ids=[0])
    out = r.results[0]["out_x"]
    return out.transpose(2, 1, 0).reshape(1, T, D)
```
